# Optimizing a Trainium2 kernel written in Bass

```python
import math
import jax, jax.numpy as jnp
from jax import lax
import numpy as np

D_MODEL = 1024
BATCH = 1
SEQ = 256
DEPTH = 2

MEM_LEN = 256
EPS = 1e-6
Q_BLOCK = 128

A_HEADS = 8
A_QK_DIM = 64
A_V_DIM = 2 * A_QK_DIM
A_WIDTH = A_HEADS * A_V_DIM
B_WIDTH = D_MODEL // 2
CONV_W = 3
C_HEADS = 12
C_DIM = 128
C_WIDTH = C_HEADS * C_DIM
X_HEADS = 4
X_DIM = 128
X_WIDTH = X_HEADS * X_DIM

EVEN_MIX = A_WIDTH + B_WIDTH + X_WIDTH
ODD_MIX = C_WIDTH + X_WIDTH
EVEN_IN = 4 * A_WIDTH + 4 * B_WIDTH + 2 * X_WIDTH
ODD_IN = 4 * C_WIDTH + C_HEADS + 2 * X_WIDTH


def rms_norm(x, g):
    xf = x.astype(jnp.float32)
    y = xf * lax.rsqrt(jnp.mean(xf * xf, axis=-1, keepdims=True) + EPS)
    return (y * g.astype(jnp.float32)).astype(x.dtype)

def alibi_slopes(n_heads):
    return jnp.asarray(np.array([2.0 ** (-8.0 * (i + 1) / n_heads) for i in range(n_heads)], dtype=np.float32))

def sweep_query_blocks(block_fn, *q_arrays):
    seq = q_arrays[0].shape[2]
    nb = seq // Q_BLOCK

    def split(a):
        a = a.reshape(a.shape[:2] + (nb, Q_BLOCK) + a.shape[3:])
        return jnp.moveaxis(a, 2, 0)

    starts = jnp.arange(nb, dtype=jnp.int32) * Q_BLOCK
    out = lax.map(lambda args: block_fn(args[0], *args[1:]), (starts,) + tuple(split(a) for a in q_arrays))
    out = jnp.moveaxis(out, 0, 2)
    return out.reshape(out.shape[:2] + (seq,) + out.shape[4:])

def differential_attention(q, k, v, q_g, k_g, lam_params, out_g, lam_init):
    bsz, seq, _ = q.shape
    q = rms_norm(q.reshape(bsz, seq, A_HEADS, 2, A_QK_DIM), q_g).transpose(0, 2, 3, 1, 4)
    k = rms_norm(k.reshape(bsz, seq, A_HEADS, 2, A_QK_DIM), k_g).transpose(0, 2, 3, 1, 4)
    v = v.reshape(bsz, seq, A_HEADS, A_V_DIM).transpose(0, 2, 1, 3)
    lp = lam_params.astype(jnp.float32)
    lam = jnp.exp(jnp.sum(lp[0] * lp[1])) - jnp.exp(jnp.sum(lp[2] * lp[3])) + lam_init
    slopes = alibi_slopes(A_HEADS)
    scale = A_QK_DIM ** -0.5
    k1, k2 = k[:, :, 0], k[:, :, 1]
    k_pos = jnp.arange(seq, dtype=jnp.int32)

    def block(start, q1b, q2b):
        q_pos = start + jnp.arange(Q_BLOCK, dtype=jnp.int32)
        dist = q_pos[:, None] - k_pos[None, :]
        causal = dist >= 0
        bias = -slopes[:, None, None] * dist.astype(jnp.float32)
        s1 = jnp.einsum('bhqd,bhkd->bhqk', q1b, k1).astype(jnp.float32) * scale + bias
        s2 = jnp.einsum('bhqd,bhkd->bhqk', q2b, k2).astype(jnp.float32) * scale + bias
        p1 = jax.nn.softmax(jnp.where(causal, s1, -jnp.inf), axis=-1)
        p2 = jax.nn.softmax(jnp.where(causal, s2, -jnp.inf), axis=-1)
        attn = (p1 - lam * p2).astype(v.dtype)
        return jnp.einsum('bhqk,bhkd->bhqd', attn, v)

    o = sweep_query_blocks(block, q[:, :, 0], q[:, :, 1])
    o = rms_norm(o, out_g) * (1.0 - lam_init)
    return o.transpose(0, 2, 1, 3).reshape(bsz, seq, A_WIDTH)

def causal_depthwise_conv(u, w, b):
    c = u.shape[-1]
    y = lax.conv_general_dilated(u, w[:, None, :].astype(u.dtype), window_strides=(1,),
                                 padding=[(CONV_W - 1, 0)],
                                 dimension_numbers=('NWC', 'WIO', 'NWC'),
                                 feature_group_count=c)
    return y + b.astype(u.dtype)

def short_gated_conv(h, c_gate, b_gate, w, b):
    return b_gate * causal_depthwise_conv(c_gate * h, w, b)

def forgetting_attention(q, k, v, f_logit, f_bias, q_g, k_g):
    bsz, seq, _ = q.shape
    q = rms_norm(q.reshape(bsz, seq, C_HEADS, C_DIM), q_g).transpose(0, 2, 1, 3)
    k = rms_norm(k.reshape(bsz, seq, C_HEADS, C_DIM), k_g).transpose(0, 2, 1, 3)
    v = v.reshape(bsz, seq, C_HEADS, C_DIM).transpose(0, 2, 1, 3)
    log_f = jax.nn.log_sigmoid(f_logit.astype(jnp.float32) + f_bias.astype(jnp.float32))
    cum = jnp.cumsum(log_f, axis=1).transpose(0, 2, 1)
    scale = C_DIM ** -0.5
    k_pos = jnp.arange(seq, dtype=jnp.int32)

    def block(start, qb, cqb):
        q_pos = start + jnp.arange(Q_BLOCK, dtype=jnp.int32)
        causal = q_pos[:, None] >= k_pos[None, :]
        s = jnp.einsum('bhqd,bhkd->bhqk', qb, k).astype(jnp.float32) * scale
        s = s + (cqb[..., :, None] - cum[:, :, None, :])
        p = jax.nn.softmax(jnp.where(causal, s, -jnp.inf), axis=-1).astype(v.dtype)
        return jnp.einsum('bhqk,bhkd->bhqd', p, v)

    o = sweep_query_blocks(block, q, cum)
    return o.transpose(0, 2, 1, 3).reshape(bsz, seq, C_WIDTH)

def memory_cross_attention(q, mem, mem_g, w_mem_kv, q_g, k_g):
    bsz, seq, _ = q.shape
    m = mem.shape[1]
    mk, mv = jnp.split(rms_norm(mem, mem_g) @ w_mem_kv, 2, axis=-1)
    q = rms_norm(q.reshape(bsz, seq, X_HEADS, X_DIM), q_g)
    mk = rms_norm(mk.reshape(bsz, m, X_HEADS, X_DIM), k_g)
    mv = mv.reshape(bsz, m, X_HEADS, X_DIM)
    s = jnp.einsum('bshd,bmhd->bhsm', q, mk).astype(jnp.float32) * (X_DIM ** -0.5)
    p = jax.nn.softmax(s, axis=-1).astype(mv.dtype)
    o = jnp.einsum('bhsm,bmhd->bshd', p, mv)
    return o.reshape(bsz, seq, X_WIDTH)

def even_layer(h, mem, layer, norm_g, w_in, w_out, a_qn, a_kn, a_lam, a_on,
               b_cw, b_cb, x_qn, x_kn, mem_g, w_mem_kv):
    u = rms_norm(h, norm_g)
    proj = u @ w_in
    cuts = np.cumsum([A_WIDTH] * 4 + [B_WIDTH] * 4 + [X_WIDTH] * 2)[:-1].tolist()
    aq, ak, av, az, bh, bc, bb, bz, xq, xz = jnp.split(proj, cuts, axis=-1)
    lam_init = 0.8 - 0.6 * math.exp(-0.3 * layer)
    ya = differential_attention(aq, ak, av, a_qn, a_kn, a_lam, a_on, lam_init)
    yb = short_gated_conv(bh, bc, bb, b_cw, b_cb)
    yx = memory_cross_attention(xq, mem, mem_g, w_mem_kv, x_qn, x_kn)
    y = jnp.concatenate([ya * jax.nn.silu(az), yb * jax.nn.silu(bz), yx * jax.nn.silu(xz)], axis=-1)
    return h + y @ w_out

def odd_layer(h, mem, norm_g, w_in, w_out, c_qn, c_kn, c_fb, x_qn, x_kn, mem_g, w_mem_kv):
    u = rms_norm(h, norm_g)
    proj = u @ w_in
    cuts = np.cumsum([C_WIDTH] * 4 + [C_HEADS] + [X_WIDTH] * 2)[:-1].tolist()
    cq, ck, cv, cz, cf, xq, xz = jnp.split(proj, cuts, axis=-1)
    yc = forgetting_attention(cq, ck, cv, cf, c_fb, c_qn, c_kn)
    yx = memory_cross_attention(xq, mem, mem_g, w_mem_kv, x_qn, x_kn)
    y = jnp.concatenate([yc * jax.nn.silu(cz), yx * jax.nn.silu(xz)], axis=-1)
    return h + y @ w_out

def first_inputs(seed: int = 0) -> dict:
    key = jax.random.key(seed)
    ks = jax.random.split(key, 32)
    it = iter(range(32))
    ne = (DEPTH + 1) // 2
    no = DEPTH // 2

    def nrm(shape, scale):
        return scale * jax.random.normal(ks[next(it)], shape, jnp.float32)

    def gain(shape):
        return 1.0 + 0.02 * jax.random.normal(ks[next(it)], shape, jnp.float32)

    return {
        "x": nrm((BATCH, SEQ, D_MODEL), 1.0),
        "mem": nrm((BATCH, MEM_LEN, D_MODEL), 1.0),
        "e_norm_g": gain((ne, D_MODEL)),
        "e_w_in": nrm((ne, D_MODEL, EVEN_IN), D_MODEL ** -0.5),
        "e_w_out": nrm((ne, EVEN_MIX, D_MODEL), EVEN_MIX ** -0.5),
        "e_a_q_norm_g": gain((ne, A_QK_DIM)),
        "e_a_k_norm_g": gain((ne, A_QK_DIM)),
        "e_a_lambda": nrm((ne, 4, A_QK_DIM), 0.1),
        "e_a_out_norm_g": gain((ne, A_V_DIM)),
        "e_b_conv_w": nrm((ne, CONV_W, B_WIDTH), CONV_W ** -0.5),
        "e_b_conv_b": nrm((ne, B_WIDTH), 0.02),
        "e_x_q_norm_g": gain((ne, X_DIM)),
        "e_x_k_norm_g": gain((ne, X_DIM)),
        "e_mem_norm_g": gain((ne, D_MODEL)),
        "e_w_mem_kv": nrm((ne, D_MODEL, 2 * X_WIDTH), D_MODEL ** -0.5),
        "o_norm_g": gain((no, D_MODEL)),
        "o_w_in": nrm((no, D_MODEL, ODD_IN), D_MODEL ** -0.5),
        "o_w_out": nrm((no, ODD_MIX, D_MODEL), ODD_MIX ** -0.5),
        "o_c_q_norm_g": gain((no, C_DIM)),
        "o_c_k_norm_g": gain((no, C_DIM)),
        "o_c_forget_b": 3.0 + nrm((no, C_HEADS), 0.5),
        "o_x_q_norm_g": gain((no, X_DIM)),
        "o_x_k_norm_g": gain((no, X_DIM)),
        "o_mem_norm_g": gain((no, D_MODEL)),
        "o_w_mem_kv": nrm((no, D_MODEL, 2 * X_WIDTH), D_MODEL ** -0.5),
    }

def first_block(x, mem, e_norm_g, e_w_in, e_w_out, e_a_q_norm_g, e_a_k_norm_g, e_a_lambda,
              e_a_out_norm_g, e_b_conv_w, e_b_conv_b, e_x_q_norm_g, e_x_k_norm_g,
              e_mem_norm_g, e_w_mem_kv, o_norm_g, o_w_in, o_w_out, o_c_q_norm_g,
              o_c_k_norm_g, o_c_forget_b, o_x_q_norm_g, o_x_k_norm_g, o_mem_norm_g,
              o_w_mem_kv):
    h = x
    for layer in range(DEPTH):
        i = layer // 2
        if layer % 2 == 0:
            h = even_layer(h, mem, layer, e_norm_g[i], e_w_in[i], e_w_out[i],
                           e_a_q_norm_g[i], e_a_k_norm_g[i], e_a_lambda[i], e_a_out_norm_g[i],
                           e_b_conv_w[i], e_b_conv_b[i], e_x_q_norm_g[i], e_x_k_norm_g[i],
                           e_mem_norm_g[i], e_w_mem_kv[i])
        else:
            h = odd_layer(h, mem, o_norm_g[i], o_w_in[i], o_w_out[i],
                          o_c_q_norm_g[i], o_c_k_norm_g[i], o_c_forget_b[i],
                          o_x_q_norm_g[i], o_x_k_norm_g[i], o_mem_norm_g[i], o_w_mem_kv[i])
    return h


N_EVEN = (DEPTH + 1) // 2
N_ODD = DEPTH // 2

HG_HEADS = 4
HG_DK = 128
HG_DV = 128
HG_WIDTH = HG_HEADS * HG_DK
HG_CHUNK = 32

CV_CH = D_MODEL - HG_HEADS * HG_DV
CV_K = 31

IN_COLS = 4 * HG_WIDTH + 2 * CV_CH

POOL_WINDOWS = (2, 4, 8, 16)
POOL_GROUPS = len(POOL_WINDOWS)
POOL_CH = D_MODEL // POOL_GROUPS

XA_HEADS = 4
XA_DH = D_MODEL // XA_HEADS

D_FF = -(-(8 * D_MODEL) // (3 * 256)) * 256

ALPHA = (2 * DEPTH) ** 0.25
BETA = (8 * DEPTH) ** -0.25
LN_EPS = 1e-5
RMS_EPS = 1e-6


def layer_norm(x, g, b):
    xf = x.astype(jnp.float32)
    mu = jnp.mean(xf, axis=-1, keepdims=True)
    var = jnp.mean(jnp.square(xf - mu), axis=-1, keepdims=True)
    y = (xf - mu) * lax.rsqrt(var + LN_EPS) * g.astype(jnp.float32) + b.astype(jnp.float32)
    return y.astype(x.dtype)

def hgrn2_chunked(q, k, v, log_f):
    B, S, H, DK = q.shape
    DV = v.shape[-1]
    nc = S // HG_CHUNK

    def to_chunks(t):
        return t.astype(jnp.float32).reshape(B, nc, HG_CHUNK, H, t.shape[-1]).transpose(0, 3, 1, 2, 4)

    q, k, v, log_f = to_chunks(q), to_chunks(k), to_chunks(v), to_chunks(log_f)
    b = jnp.cumsum(log_f, axis=3)
    b_last = b[:, :, :, -1:, :]
    q_t = q * jnp.exp(b)
    k_t = k * jnp.exp(-b)
    causal = jnp.tril(jnp.ones((HG_CHUNK, HG_CHUNK), dtype=bool))
    scores = jnp.einsum('bhntd,bhnsd->bhnts', q_t, k_t)
    scores = jnp.where(causal, scores, 0.0)
    o_intra = jnp.einsum('bhnts,bhnsv->bhntv', scores, v)
    k_end = k * jnp.exp(b_last - b)
    d_state = jnp.einsum('bhnsd,bhnsv->bhndv', k_end, v)
    decay = jnp.exp(b_last[:, :, :, 0, :])

    def step(state, inp):
        dec, ds = inp
        return dec[..., None] * state + ds, state

    s0 = jnp.zeros((B, H, DK, DV), jnp.float32)
    _, s_start = lax.scan(step, s0, (jnp.moveaxis(decay, 2, 0), jnp.moveaxis(d_state, 2, 0)))
    s_start = jnp.moveaxis(s_start, 0, 2)
    o_inter = jnp.einsum('bhntd,bhndv->bhntv', q_t, s_start)
    o = o_intra + o_inter
    return o.transpose(0, 2, 3, 1, 4).reshape(B, S, H, DV)

def hybrid_ab_mixer(x, w_in, lb, hg_norm_g, cv_w, cv_b, cv_ln_g, cv_ln_b, w_out):
    B, S, _ = x.shape
    h = x @ w_in
    q, f_pre, i_v, g, a, a_gate = jnp.split(
        h, [HG_WIDTH, 2 * HG_WIDTH, 3 * HG_WIDTH, 4 * HG_WIDTH, 4 * HG_WIDTH + CV_CH], axis=-1)

    lb = lb.astype(jnp.float32)
    f_pre = f_pre.astype(jnp.float32)
    f = lb + (1.0 - lb) * jax.nn.sigmoid(f_pre)
    k = (1.0 - lb) * jax.nn.sigmoid(-f_pre)
    log_f = jnp.log(f)
    heads = lambda t: t.reshape(B, S, HG_HEADS, -1)
    o = hgrn2_chunked(heads(q), heads(k), heads(i_v), heads(log_f))
    o = o * lax.rsqrt(jnp.mean(jnp.square(o), axis=-1, keepdims=True) + RMS_EPS)
    o = o.reshape(B, S, HG_HEADS * HG_DV) * hg_norm_g.astype(jnp.float32) * jax.nn.silu(g.astype(jnp.float32))

    u = a * jax.nn.sigmoid(a_gate)
    u = lax.conv_general_dilated(
        u, cv_w.astype(u.dtype), window_strides=(1,), padding=[(CV_K - 1, 0)],
        dimension_numbers=('NWC', 'WIO', 'NWC'), feature_group_count=CV_CH) + cv_b
    u = jax.nn.silu(layer_norm(u, cv_ln_g, cv_ln_b))

    y = jnp.concatenate([o.astype(x.dtype), u.astype(x.dtype)], axis=-1)
    return y @ w_out

def multiscale_pool_mixer(x, pool_w, pool_scale):
    B, S, _ = x.shape
    xg = x.astype(jnp.float32).reshape(B, S, POOL_GROUPS, POOL_CH)
    cs = jnp.cumsum(xg, axis=1)
    pos = jnp.arange(1, S + 1, dtype=jnp.float32)
    feats = []
    for gi, w in enumerate(POOL_WINDOWS):
        c = cs[:, :, gi]
        lagged = jnp.pad(c, ((0, 0), (w, 0), (0, 0)))[:, :S]
        mean = (c - lagged) / jnp.minimum(pos, float(w))[:, None]
        feats.append(mean - xg[:, :, gi])
    p = jnp.stack(feats, axis=2).astype(x.dtype)
    y = jnp.einsum('bsgc,gcd->bsgd', p, pool_w).reshape(B, S, D_MODEL)
    return y * pool_scale

def memory_cross_attention_2(x, mem_n, w_q, w_k, w_v, w_o):
    B, S, _ = x.shape
    q = (x @ w_q).reshape(B, S, XA_HEADS, XA_DH)
    k = (mem_n @ w_k).reshape(B, -1, XA_HEADS, XA_DH)
    v = (mem_n @ w_v).reshape(B, -1, XA_HEADS, XA_DH)
    s = jnp.einsum('bshd,bmhd->bhsm', q, k).astype(jnp.float32) * (XA_DH ** -0.5)
    p = jax.nn.softmax(s, axis=-1).astype(x.dtype)
    o = jnp.einsum('bhsm,bmhd->bshd', p, v).reshape(B, S, D_MODEL)
    return o @ w_o

def swiglu_ffn(x, w_gate, w_up, w_down):
    return (jax.nn.silu(x @ w_gate) * (x @ w_up)) @ w_down

def second_inputs(seed: int = 0) -> dict:
    key = jax.random.key(seed)
    ks = jax.random.split(key, 32)
    f32 = jnp.float32
    nrm = lambda k, shape, scale: jax.random.normal(k, shape, f32) * scale
    gain = lambda k, shape: 1.0 + 0.02 * jax.random.normal(k, shape, f32)
    bias = lambda k, shape: 0.02 * jax.random.normal(k, shape, f32)
    d = D_MODEL
    return {
        "x": jax.random.normal(ks[0], (BATCH, SEQ, d), f32),
        "mem": jax.random.normal(ks[1], (BATCH, MEM_LEN, d), f32),
        "lb_param": nrm(ks[2], (DEPTH + 1, HG_WIDTH), 0.1),
        "mem_ln_g": gain(ks[3], (d,)),
        "mem_ln_b": bias(ks[4], (d,)),
        "ab_w_in": nrm(ks[5], (N_EVEN, d, IN_COLS), d ** -0.5),
        "hg_norm_g": gain(ks[6], (N_EVEN, HG_HEADS * HG_DV)),
        "cv_w": nrm(ks[7], (N_EVEN, CV_K, 1, CV_CH), CV_K ** -0.5),
        "cv_b": bias(ks[8], (N_EVEN, CV_CH)),
        "cv_ln_g": gain(ks[9], (N_EVEN, CV_CH)),
        "cv_ln_b": bias(ks[10], (N_EVEN, CV_CH)),
        "ab_w_out": nrm(ks[11], (N_EVEN, d, d), BETA * d ** -0.5),
        "pool_w": nrm(ks[12], (N_ODD, POOL_GROUPS, POOL_CH, POOL_CH), BETA * POOL_CH ** -0.5),
        "pool_scale": gain(ks[13], (N_ODD, d)),
        "ln_mix_g": gain(ks[14], (DEPTH, d)),
        "ln_mix_b": bias(ks[15], (DEPTH, d)),
        "xa_wq": nrm(ks[16], (DEPTH, d, d), d ** -0.5),
        "xa_wk": nrm(ks[17], (DEPTH, d, d), d ** -0.5),
        "xa_wv": nrm(ks[18], (DEPTH, d, d), d ** -0.5),
        "xa_wo": nrm(ks[19], (DEPTH, d, d), BETA * d ** -0.5),
        "ln_xa_g": gain(ks[20], (DEPTH, d)),
        "ln_xa_b": bias(ks[21], (DEPTH, d)),
        "ffn_wg": nrm(ks[22], (DEPTH, d, D_FF), d ** -0.5),
        "ffn_wu": nrm(ks[23], (DEPTH, d, D_FF), d ** -0.5),
        "ffn_wd": nrm(ks[24], (DEPTH, D_FF, d), BETA * D_FF ** -0.5),
        "ln_ffn_g": gain(ks[25], (DEPTH, d)),
        "ln_ffn_b": bias(ks[26], (DEPTH, d)),
    }

def second_block(x, mem, lb_param, mem_ln_g, mem_ln_b, ab_w_in, hg_norm_g, cv_w, cv_b,
              cv_ln_g, cv_ln_b, ab_w_out, pool_w, pool_scale, ln_mix_g, ln_mix_b,
              xa_wq, xa_wk, xa_wv, xa_wo, ln_xa_g, ln_xa_b, ffn_wg, ffn_wu, ffn_wd,
              ln_ffn_g, ln_ffn_b):
    lb_all = jnp.cumsum(jax.nn.softmax(lb_param.astype(jnp.float32), axis=0), axis=0)
    mem_n = layer_norm(mem, mem_ln_g, mem_ln_b)
    for l in range(DEPTH):
        if l % 2 == 0:
            e = l // 2
            y = hybrid_ab_mixer(x, ab_w_in[e], lb_all[l], hg_norm_g[e], cv_w[e], cv_b[e],
                                cv_ln_g[e], cv_ln_b[e], ab_w_out[e])
        else:
            o = l // 2
            y = multiscale_pool_mixer(x, pool_w[o], pool_scale[o])
        x = layer_norm(ALPHA * x + y, ln_mix_g[l], ln_mix_b[l])
        y = memory_cross_attention_2(x, mem_n, xa_wq[l], xa_wk[l], xa_wv[l], xa_wo[l])
        x = layer_norm(ALPHA * x + y, ln_xa_g[l], ln_xa_b[l])
        y = swiglu_ffn(x, ffn_wg[l], ffn_wu[l], ffn_wd[l])
        x = layer_norm(ALPHA * x + y, ln_ffn_g[l], ln_ffn_b[l])
    return x


def setup_inputs(seed=0):
    out = dict(first_inputs(seed))
    for name, value in second_inputs(seed + 1).items():
        if name != "x":
            out[name + "_2"] = value
    return out


def reference(
    x, mem, e_norm_g, e_w_in, e_w_out, e_a_q_norm_g, e_a_k_norm_g, e_a_lambda, e_a_out_norm_g,
    e_b_conv_w, e_b_conv_b, e_x_q_norm_g, e_x_k_norm_g, e_mem_norm_g, e_w_mem_kv, o_norm_g,
    o_w_in, o_w_out, o_c_q_norm_g, o_c_k_norm_g, o_c_forget_b, o_x_q_norm_g, o_x_k_norm_g,
    o_mem_norm_g, o_w_mem_kv, mem_2, lb_param_2, mem_ln_g_2, mem_ln_b_2, ab_w_in_2, hg_norm_g_2,
    cv_w_2, cv_b_2, cv_ln_g_2, cv_ln_b_2, ab_w_out_2, pool_w_2, pool_scale_2, ln_mix_g_2,
    ln_mix_b_2, xa_wq_2, xa_wk_2, xa_wv_2, xa_wo_2, ln_xa_g_2, ln_xa_b_2, ffn_wg_2, ffn_wu_2,
    ffn_wd_2, ln_ffn_g_2, ln_ffn_b_2,
):
    x = first_block(
        x, mem, e_norm_g, e_w_in, e_w_out, e_a_q_norm_g, e_a_k_norm_g, e_a_lambda,
        e_a_out_norm_g, e_b_conv_w, e_b_conv_b, e_x_q_norm_g, e_x_k_norm_g, e_mem_norm_g,
        e_w_mem_kv, o_norm_g, o_w_in, o_w_out, o_c_q_norm_g, o_c_k_norm_g, o_c_forget_b,
        o_x_q_norm_g, o_x_k_norm_g, o_mem_norm_g, o_w_mem_kv,
    )
    return second_block(
        x, mem_2, lb_param_2, mem_ln_g_2, mem_ln_b_2, ab_w_in_2, hg_norm_g_2, cv_w_2, cv_b_2,
        cv_ln_g_2, cv_ln_b_2, ab_w_out_2, pool_w_2, pool_scale_2, ln_mix_g_2, ln_mix_b_2,
        xa_wq_2, xa_wk_2, xa_wv_2, xa_wo_2, ln_xa_g_2, ln_xa_b_2, ffn_wg_2, ffn_wu_2, ffn_wd_2,
        ln_ffn_g_2, ln_ffn_b_2,
    )


_drawn_inputs = setup_inputs


def setup_inputs(seed=0):
    import zlib

    import numpy as np

    out = dict(_drawn_inputs(seed))
    spreads = {}
    factors = {'e_norm_g': 3.073,
     'e_a_q_norm_g': 8.0,
     'e_a_k_norm_g': 8.0,
     'e_a_out_norm_g': 7.713,
     'e_b_conv_b': 8.0,
     'e_x_q_norm_g': 8.0,
     'e_x_k_norm_g': 8.0,
     'e_mem_norm_g': 8.0,
     'o_norm_g': 8.0,
     'o_c_q_norm_g': 8.0,
     'o_c_k_norm_g': 8.0,
     'o_x_q_norm_g': 8.0,
     'o_x_k_norm_g': 8.0,
     'o_mem_norm_g': 8.0,
     'lb_param_2': 6.399,
     'mem_ln_g_2': 8.0,
     'mem_ln_b_2': 5.507,
     'hg_norm_g_2': 8.0,
     'cv_b_2': 64.0,
     'cv_ln_g_2': 200.0,
     'cv_ln_b_2': 200.0,
     'pool_scale_2': 8.0}
    for name, (base, spread) in spreads.items():
        noise = np.random.default_rng([zlib.crc32(name.encode()), seed]).standard_normal(out[name].shape)
        drawn = base * np.exp(spread * noise) if base else spread * noise
        out[name] = __import__('jax').numpy.asarray(drawn.astype(out[name].dtype))
    for name, factor in factors.items():
        out[name] = (out[name] * factor).astype(out[name].dtype)
    return out
```

```python
from contextlib import ExitStack

import numpy as np

import concourse.bass as bass
from concourse import mybir

F32 = mybir.dt.float32
F32R = mybir.dt.float32r
ALU = mybir.AluOpType
ACT = mybir.ActivationFunctionType
AX = mybir.AxisListType

P = 128
SEQ = 256
D = 1024
EPS = 1e-6
LN_EPS = 1e-5
A_HEADS, B_W, C_HEADS, X_HEADS, G_HEADS = 8, 512, 12, 4, 4
D_FF = 2816
CONV_W = 3
CV_K = 31
CV_PE = 6
PE_FIRST = 1
HG_CHUNK = 32
N_CHUNK = SEQ // HG_CHUNK
POOL_WINDOWS = (2, 4, 8, 16)
ALPHA = 4.0 ** 0.25
LAM_INIT = 0.8 - 0.6
MASKED = -1e30
FFN_STEPS = D_FF // SEQ

PHASES = [
    ("e_kv", "K8", 4), ("e_conv", "K8", 8), ("e_nat", "K8", 20), ("e_out", "DN", 8),
    ("o_kv", "K8", 4), ("o_nat", "K8", 28), ("o_out", "DN", 8),
    ("ab_t", "K8", 8), ("ab_nat", "K8", 4), ("xk0", "K8", 4), ("xv0", "K8", 4), ("ab_out", "DN", 4),
    ("xq0", "K8", 4), ("xo0", "DN", 4), ("xk1", "K8", 4), ("ffn0", "FFN", 3 * FFN_STEPS),
    ("xv1", "K8", 4), ("xq1", "K8", 4), ("xo1", "DN", 4), ("ffn1", "FFN", 3 * FFN_STEPS),
]
UNIT0, BANK0 = {}, {}
_u = _k = 0
for _name, _kind, _n in PHASES:
    UNIT0[_name], BANK0[_name] = _u, _k
    _u += _n
    _k += {"K8": _n, "DN": 0, "FFN": FFN_STEPS}[_kind]
UNITS = _u
COUNT = {name: n for name, _, n in PHASES}


def unit_end(name):
    return 2 * (UNIT0[name] + COUNT[name])


HEADS = ([("A", h) for h in range(A_HEADS)] + [("X", h) for h in range(X_HEADS)]
         + [("C", h) for h in range(C_HEADS)] + [("Y", h) for h in range(X_HEADS)]
         + [("G", h) for h in range(G_HEADS)] + [("G", h) for h in range(G_HEADS)])
PASS = {"e": (0, 12), "o": (12, 28), "x0": (28, 32), "x1": (32, 36)}
LAG = 5
BESIDE = {"e": ("e_nat", 10, A_HEADS + 2), "o": ("o_nat", 14, C_HEADS + 2), "x0": (None, 0, 0), "x1": (None, 0, 0)}


def v_unit(kind, hd):
    name, before, _ = BESIDE["e" if kind == "A" else "o"]
    return BANK0[name] + before + 2 * (hd // 2) + 1


def z_unit(kind, hd):
    name, before, _ = BESIDE["e" if kind in "AX" else "o"]
    first = {"A": 1, "C": 1, "X": A_HEADS, "Y": C_HEADS}[kind]
    return BANK0[name] + before + first + (2 if kind in "AC" else 1) * (hd // 2) + 1

G1_ROWS = [("e_norm_g", 8), ("e_mem_norm_g", 8), ("o_norm_g", 8), ("o_mem_norm_g", 8),
           ("mem_ln_g_2", 8), ("mem_ln_b_2", 8), ("mix_g", 16), ("mix_b", 16), ("xa_g", 16), ("xa_b", 16)]
G2_ROWS = [("e_b_conv_w", 12), ("e_b_conv_b", 4), ("cv_b_2", 4), ("cv_ln_g_2", 4), ("cv_ln_b_2", 4),
           ("lb_param_2", 12), ("aq", 1), ("ak", 1), ("exq", 1), ("exk", 1), ("cq", 1), ("ck", 1),
           ("oxq", 1), ("oxk", 1)]
GCOL = {}
_c = 0
for _n, _r in G1_ROWS:
    GCOL[_n] = _c
    _c += _r
G1_N = _c
for _n, _r in G2_ROWS:
    GCOL[_n] = _c
    _c += _r
G2_N = _c - G1_N
GCOL["cv_w"] = _c
G3_N = CV_K * 4
G_N = _c + G3_N

POWS = [("mem", 2), ("x", 2), ("mk_e", 8), ("aq", 32), ("ak", 32), ("xq_e", 8), ("h1", 2), ("mk_o", 8),
        ("cq", 24), ("ck", 24), ("xq_o", 8), ("mem2", 2), ("hg", 8), ("mix0", 2), ("xa0", 2), ("ffn0", 2),
        ("mix1", 2), ("xa1", 2), ("ffn1", 2)]
POW_AT, POW_N = {}, {}
_c = 0
for _i, (_n, _w) in enumerate(POWS):
    POW_AT[_n] = (_c, _w)
    POW_N[_n] = _i + 1
    _c += _w
POW_W = _c

C_ID, C_DIST, C_MASK, C_TRI, C_HG, C_SCAN = 0, 128, 512, 896, 1024, 1152
C_N = 1408


def shape_constants():
    q, k = np.arange(P)[:, None], np.arange(P)[None, :]
    c = np.zeros((P, C_N), np.float32)
    c[:, C_ID:C_ID + P] = q == k
    dist = np.concatenate([q - k, q + P - np.arange(SEQ)[None, :]], 1)
    c[:, C_DIST:C_DIST + 384] = np.where(dist >= 0, -dist, MASKED)
    c[:, C_MASK:C_MASK + 384] = np.where(dist >= 0, 0.0, MASKED)
    c[:, C_TRI:C_TRI + P] = q <= k
    c[:, C_HG:C_HG + P] = (q <= k) & (q // HG_CHUNK == k // HG_CHUNK)
    c[:, C_SCAN:C_SCAN + SEQ] = np.arange(SEQ)[None, :] % HG_CHUNK != 0
    s, t = np.arange(SEQ)[:, None], np.arange(SEQ)[None, :]
    pm = np.zeros((P, len(POOL_WINDOWS), 384), np.float32)
    for g, w in enumerate(POOL_WINDOWS):
        m = np.where((s <= t) & (s > t - w), 1.0 / np.minimum(t + 1, w), 0.0) - (s == t)
        pm[:, g, 0:SEQ] = m[0:P]
        pm[:, g, SEQ:384] = m[P:SEQ, P:SEQ]
    return c, pm.reshape(P, -1)


def build_program(nc, t, out):
    with ExitStack() as ctx:
        def sb(name, words, dt=F32):
            return ctx.enter_context(nc.sbuf_tensor(name, [P, words], dt))

        def sem(name):
            return ctx.enter_context(nc.semaphore(name))

        h = sb("h", 2 * D)
        u_hi, u_lo = sb("u_hi", 8 * SEQ, F32R), sb("u_lo", 8 * SEQ, F32R)
        y_hi, y_lo = sb("y_hi", 16 * SEQ, F32R), sb("y_lo", 16 * SEQ, F32R)
        w_raw = sb("w_raw", 2 * 2048)
        w_hi, w_lo = sb("w_hi", 2 * 2048, F32R), sb("w_lo", 2 * 2048, F32R)
        nat = sb("nat", 14 * D)
        mkv = sb("mkv", 4 * D)
        att = sb("att", 4992)
        cst = sb("cst", C_N)
        gT = sb("gT", G_N)
        bc = sb("bc", P + 12)
        qs = sb("qs", 4)
        pow_in, pow_out = sb("pow_in", POW_W), sb("pow_out", POW_W)
        mhalf = sb("mhalf", 32)
        ones = sb("ones", P)
        small = sb("small", 256)
        cf_hi, cf_lo = sb("cf_hi", 96, F32R), sb("cf_lo", 96, F32R)
        bank = [ctx.enter_context(nc.psum_tensor(f"bank{i}", [P, 512], F32)) for i in range(8)]
        SC, PTB, OB, TRB, YTB = (2, 3), 4, 5, 6, 7
        DOWN = (2, 3, 4, 5)

        ident = cst[:, C_ID:C_ID + P]

        def two(ap, w):
            return ap.rearrange("p (m w) -> p m w", w=w)

        def tv(ap):
            return ap.rearrange("p (k n) -> p k n", n=SEQ)

        hv = two(h[:, :], D)
        uh, ul, yh_, yl_ = tv(u_hi[:, :]), tv(u_lo[:, :]), tv(y_hi[:, :]), tv(y_lo[:, :])
        nrm = two(att[:, 0:2 * D], D)
        vT = tv(att[:, 2 * D:4 * D])
        memA = tv(mkv[:, 2 * D:4 * D])
        MKT = tv(mkv[:, 0:D])
        MV = two(mkv[:, D:2 * D], 512)
        KT2 = tv(mkv[:, 0:2 * D])
        V2 = two(mkv[:, 2 * D:4 * D], D)

        def region(at, w):
            return two(nat[:, at:at + 2 * w], w)

        eQ, eK, eV, eZ = (region(2048 * i, D) for i in range(4))
        eXQ, eXZ = region(8192, 512), region(9216, 512)
        eBH, eBC, eBB, eBZ = (tv(nat[:, 10240 + 1024 * i:11264 + 1024 * i]) for i in range(4))
        MKN = region(6144, 512)
        oQ, oK, oV, oZ = (region(3072 * i, 1536) for i in range(4))
        oXQ, oXZ = region(12288, 512), region(13312, 512)
        HA, HG, HQ, SF, SN = (tv(nat[:, 1024 * i:1024 * i + 1024]) for i in range(5))
        HV, GG = region(5120, 512), region(6144, 512)
        LF, HB, KT = (tv(nat[:, 7168 + 1024 * i:8192 + 1024 * i]) for i in range(3))
        KN, STM = region(0, 512), region(1024, 512)
        ON, SQ = region(3072, 512), region(4096, 512)
        STATE = nat[:, 10240:14336].rearrange("p (n w) -> p n w", w=512)
        UP = att[:, 0:4 * (SEQ + 30)].rearrange("p (k n) -> p k n", n=SEQ + 30)
        CA, CS = tv(att[:, 1152:2176]), tv(att[:, 2176:3200])
        CR = att[:, 3200:3456]
        HGB = att[:, 3456:3968]
        DIAG = [att[:, 3968 + 512 * i:4480 + 512 * i] for i in range(2)]
        LNG, LNB = nat[:, 0:D], nat[:, D:2 * D]
        XQT = tv(nat[:, 2048:4096])
        PSC = nat[:, 4096:5120]
        SG, HF = nat[:, 6144:7168], nat[:, 7168:8192]
        PM = nat[:, 8192:9728].rearrange("p (g n) -> p g n", n=384)
        PW = tv(nat[:, 9728:11776])
        PT_ = tv(nat[:, 11776:13824])
        qk = [att[:, 512 * i:512 * i + 512] for i in range(2)]
        Sb = [att[:, 1024 + 768 * i:1792 + 768 * i] for i in range(2)]
        pT = [att[:, 2560 + 512 * i:3072 + 512 * i] for i in range(2)]
        ys = [att[:, 3584 + 512 * i:4096 + 512 * i] for i in range(2)]
        tp = att[:, 4608:4992]
        rows = nat[:, 13312:13696]
        msq = nat[:, 7168:8192]
        cf_raw = tp[:, 256:352]
        zrow = nat[:, 5120:5632]
        nmax = [small[:, 4 * i:4 * i + 4] for i in range(2)]
        rsum = [small[:, 8 + 4 * i:12 + 4 * i] for i in range(2)]
        rinv = [small[:, 184 + 4 * i:188 + 4 * i] for i in range(4)]
        plam = [small[:, 24 + 2 * i:26 + 2 * i] for i in range(2)]
        ssq = [small[:, 28 + 4 * i:30 + 4 * i] for i in range(2)]
        rout = [small[:, 30 + 4 * i:32 + 4 * i] for i in range(2)]
        nlam = small[:, 36:37]
        bn6 = small[:, 40:64]
        mv = small[:, 64:68].rearrange("p (m two) -> p m two", two=2)
        lamw = small[:, 68:72]
        cfl = small[:, 72:96]
        cft = small[:, 96:120]
        lb = small[:, 120:124]
        oml = small[:, 124:128]
        lbe = small[:, 128:140]
        lbm = small[:, 140:144]
        lbs = small[:, 144:148]
        decay = small[:, 148:180]
        epsc = small[:, 180:181]
        cumT = tp[0:12, 0:SEQ]

        w_landed = [sem("w_landed0"), sem("w_landed1")]
        hi_done, lo_done = sem("hi_done"), sem("lo_done")
        half_done = sem("half_done")
        tile0_out = sem("tile0_out")
        evacuated = sem("evacuated")
        x_in, mem_in, cst_in, mem2_in = sem("x_in"), sem("mem_in"), sem("cst_in"), sem("mem2_in")
        rows2_in, zrow_done, ff_a, ff_b = sem("rows2_in"), sem("zrow_done"), sem("ff_a"), sem("ff_b")
        rows_in, bc_in, lam_in, hgb_in = sem("rows_in"), sem("bc_in"), sem("lam_in"), sem("hgb_in")
        cf_in, pool_in, ln_in = sem("cf_in"), sem("pool_in"), sem("ln_in")
        init_done = sem("init_done")
        pow_asked, pow_done = sem("pow_asked"), sem("pow_done")
        dve_step, act_step, pool_step = sem("dve_step"), sem("act_step"), sem("pool_step")
        gains_t, gains_ready = sem("gains_t"), sem("gains_ready")
        lam_sum, lam_exp = sem("lam_sum"), sem("lam_exp")
        nrm_ready = sem("nrm_ready")
        tT, tV, tL = sem("tT"), sem("tV"), sem("tL")
        memG_v, memG_ready = sem("memG_v"), sem("memG_ready")
        mkn_ready, mk_t, mk_ready = sem("mkn_ready"), sem("mk_t"), sem("mk_ready")
        conv_ready, conv_hi, conv_lo = sem("conv_ready"), sem("conv_hi"), sem("conv_lo")
        qk_ready = sem("qk_ready")
        gate_ready = sem("gate_ready")
        h_ready = sem("h_ready")
        cf_split, cf_mm, cf_act, cf_dve, cum_mm, cum_ready = (
            sem(n) for n in ("cf_split", "cf_mm", "cf_act", "cf_dve", "cum_mm", "cum_ready"))
        a_tr, a_qk, a_sc, a_mx, a_ex, a_pn, a_pt, a_pe, a_pv, a_sq, a_rp, a_yn, a_yt, a_yh, a_yl = (
            sem(n) for n in ("a_tr", "a_qk", "a_sc", "a_mx", "a_ex", "a_pn", "a_pt", "a_pe", "a_pv",
                             "a_sq", "a_rp", "a_yn", "a_yt", "a_yh", "a_yl"))
        hg_f, hg_ln, hg_b, hg_e, hg_k, hg_tr, hg_kn, hg_st, hg_sm, hg_ds, hg_s, hg_o, hg_on, hg_y, hg_yt, \
            hg_yh, hg_yl = (sem("hg_" + n) for n in ("f", "ln", "b", "e", "k", "tr", "kn", "st", "sm", "ds",
                                                      "s", "o", "on", "y", "yt", "yh", "yl"))
        cv_mu, cv_c, cv_var, cv_sd, cv_x, cv_v = (sem("cv_" + n) for n in ("mu", "c", "var", "sd", "x", "v"))
        up_ready = sem("up_ready")
        diag_ready, diag_used = sem("diag_ready"), sem("diag_used")
        lb_exp, lb_sub = sem("lb_exp"), sem("lb_sub")
        h_split = sem("h_split")
        pm_mm, pm_ev, pm_out = sem("pm_mm"), sem("pm_ev"), sem("pm_out")
        stored = sem("stored")

        block = ctx.enter_context(nc.Block())

        @block.sync
        def _(sp):
            def load(u_slot, first, landed_wait, src):
                if not first:
                    sp.wait_ge(lo_done, landed_wait)
                sp.dma_start(w_raw[:, 2048 * u_slot:2048 * u_slot + 2048].rearrange(
                    "p (k n) -> p k n", n=src.shape[-1]), src).then_inc(w_landed[u_slot], 16)

            def k8(base, w, c0, n):
                def unit(base_j, col, i4):
                    src = w[:, bass.ds(col, SEQ)] if i4 is not None else w[:, col:col + SEQ]
                    v = 2 * base_j - 2
                    load(base_j % 2, base_j < 2, v if i4 is None else i4 + v,
                         src.rearrange("(k p) n -> p k n", p=P))
                if base < 2 or n < 4:
                    for j in range(n):
                        unit(base + j, c0 + SEQ * j, None)
                else:
                    with sp.Fori(0, n // 2) as i:
                        for j in range(2):
                            unit(base + j, 2 * SEQ * i + (c0 + SEQ * j), 4 * i)
                return base + n

            def dn(base, w, n):
                for j in range(n):
                    load((base + j) % 2, False, 2 * (base + j) - 2,
                         w[SEQ * j:SEQ * j + SEQ, :].rearrange("(k p) n -> p k n", p=P))

            def ffn(base, wg, wu, wd):
                def gu(u, s, reg):
                    for n, w in ((0, wg), (1, wu)):
                        v = 2 * (u + n) - 2
                        src = w[:, bass.ds(512 * reg + SEQ * s, SEQ)] if reg is not None else w[:, SEQ * s:SEQ * s + SEQ]
                        load((u + n) % 2, False, v if reg is None else 12 * reg + v,
                             src.rearrange("(k p) n -> p k n", p=P))

                def down(u, s, reg):
                    v = 2 * u - 2
                    src = wd[bass.ds(512 * reg + SEQ * s, SEQ), :] if reg is not None else wd[SEQ * s:SEQ * s + SEQ, :]
                    load(u % 2, False, v if reg is None else 12 * reg + v,
                         src.rearrange("(k p) n -> p k n", p=P))
                gu(base, 0, None)
                with sp.Fori(0, (FFN_STEPS - 1) // 2) as i:
                    for j in range(2):
                        gu(base + 2 + 3 * j, 1 + j, i)
                        down(base + 4 + 3 * j, j, i)
                down(base + 3 * FFN_STEPS - 1, FFN_STEPS - 1, None)

            sp.dma_start(two(att[:, 0:2 * D], D), t["mem"][0].rearrange("(m p) n -> p m n", p=P)).then_inc(mem_in, 16)
            for j in range(2):
                k8(j, t["e_w_mem_kv"][0], SEQ * j, 1)
            sp.dma_start(hv, t["x"][0].rearrange("(m p) n -> p m n", p=P)).then_inc(x_in, 16)

            def row(r0, c, src, width=P):
                sp.dma_start(rows[r0:r0 + src.shape[0], c:c + width], src).then_inc(rows2_in, 16)
            row(0, P, t["e_b_conv_w"][0].rearrange("w (k p) -> (w k) p", p=P))
            row(12, P, t["e_b_conv_b"][0].rearrange("(k p) -> k p", p=P))
            for i, name in enumerate(("cv_b_2", "cv_ln_g_2", "cv_ln_b_2")):
                row(16 + 4 * i, P, t[name][0].rearrange("(k p) -> k p", p=P))
            row(28, P, t["lb_param_2"].rearrange("w (k p) -> (w k) p", p=P))
            for i, name in enumerate(("e_a_q_norm_g", "e_a_k_norm_g")):
                row(40 + i, P, t[name], 64)
                row(40 + i, P + 64, t[name], 64)
            for i, name in enumerate(("e_x_q_norm_g", "e_x_k_norm_g", "o_c_q_norm_g", "o_c_k_norm_g",
                                      "o_x_q_norm_g", "o_x_k_norm_g")):
                row(42 + i, P, t[name])
            row(0, 2 * P, t["cv_w_2"][0].rearrange("w o (k p) -> (w o k) p", p=P))
            for j in range(2, 4):
                k8(j, t["e_w_mem_kv"][0], SEQ * j, 1)
            u = 4
            w = t["e_w_in"][0]
            u = k8(u, w, 4096, 8)
            u = k8(u, w, 0, 8)
            u = k8(u, w, 6144, 2)
            for j in range(A_HEADS // 2):
                u = k8(u, w, 2048 + SEQ * j, 1)
                u = k8(u, w, 3072 + SEQ * j, 1)
            u = k8(u, w, 6656, 2)
            dn(u, t["e_w_out"][0], 8)
            u = k8(UNIT0["o_kv"], t["o_w_mem_kv"][0], 0, 4)
            w = t["o_w_in"][0]
            u = k8(u, w, 0, 12)
            u = k8(u, w, 6156, 2)
            for j in range(C_HEADS // 2):
                u = k8(u, w, 3072 + SEQ * j, 1)
                u = k8(u, w, 4608 + SEQ * j, 1)
            u = k8(u, w, 6668, 2)
            dn(u, t["o_w_out"][0], 8)
            w = t["ab_w_in_2"][0]
            u = k8(UNIT0["ab_t"], w, 2048, 4)
            u = k8(u, w, 512, 2)
            u = k8(u, w, 0, 2)
            u = k8(u, w, 1024, 4)
            u = k8(u, t["xa_wk_2"][0], 0, 4)
            u = k8(u, t["xa_wv_2"][0], 0, 4)
            dn(u, t["ab_w_out_2"][0], 4)
            u = k8(UNIT0["xq0"], t["xa_wq_2"][0], 0, 4)
            dn(u, t["xa_wo_2"][0], 4)
            k8(UNIT0["xk1"], t["xa_wk_2"][1], 0, 4)
            ffn(UNIT0["ffn0"], t["ffn_wg_2"][0], t["ffn_wu_2"][0], t["ffn_wd_2"][0])
            k8(UNIT0["xv1"], t["xa_wv_2"][1], 0, 4)
            k8(UNIT0["xq1"], t["xa_wq_2"][1], 0, 4)
            dn(UNIT0["xo1"], t["xa_wo_2"][1], 4)
            ffn(UNIT0["ffn1"], t["ffn_wg_2"][1], t["ffn_wu_2"][1], t["ffn_wd_2"][1])
            for m in range(2):
                sp.wait_ge(h_ready, 8 + m)
                sp.dma_start(out[0].rearrange("(m p) n -> p m n", p=P)[:, m], hv[:, m]).then_inc(stored, 16)
            sp.wait_ge(stored, 32)

        @block.tensor
        def _(pe):
            def passes(out_ap, pairs, start, stop_, last=False):
                (ah, al), (bh, bl) = pairs
                pe.matmul(out_ap, ah, bh, start=start, stop=False, skip_group_check=True)
                pe.matmul(out_ap, ah, bl, start=False, stop=False, skip_group_check=True)
                return pe.matmul(out_ap, al, bh, start=False, stop=stop_, skip_group_check=True)

            def k8_unit(slot, bk, xh, xl, weights_stationary, wait_lo, wait_bank, fresh=None):
                for half in range(2):
                    if fresh is not None:
                        pe.wait_ge(tL, fresh - 4 + 4 * half)
                    pe.wait_ge(lo_done, wait_lo + half)
                    if half == 0 and wait_bank is not None:
                        pe.wait_ge(evacuated, wait_bank)
                    for m in range(2):
                        for k in range(4 * half, 4 * half + 4):
                            at = 2048 * slot + SEQ * k
                            o = bank[bk][:, SEQ * m:SEQ * m + SEQ]
                            first = half == 0 and m == 0 and k == 0
                            end = k == 7
                            if weights_stationary:
                                a = at + P * m
                                mm = passes(o, ((w_hi[:, a:a + P], w_lo[:, a:a + P]), (xh[:, k, :], xl[:, k, :])),
                                            first, end)
                            else:
                                mm = passes(o, ((xh[:, k, P * m:P * m + P], xl[:, k, P * m:P * m + P]),
                                                (w_hi[:, at:at + SEQ], w_lo[:, at:at + SEQ])), first, end)
                    mm.then_inc(half_done, 1)

            def k8_phase(name, xh, xl, weights_stationary, n=None, skip=0, fresh=None):
                base, kb = UNIT0[name] + skip, BANK0[name] + skip
                n = COUNT[name] if n is None else n
                if n == 2 or fresh is not None:
                    for j in range(2):
                        k8_unit((base + j) % 2, (kb + j) % 2, xh, xl, weights_stationary, 2 * (base + j) + 1,
                                kb + j - 1 if kb + j > 1 else None, fresh if j == 0 else None)
                    if n > 2:
                        k8_phase(name, xh, xl, weights_stationary, n - 2, skip + 2)
                    return
                with pe.Fori(0, n // 2) as i:
                    for j in range(2):
                        k8_unit((base + j) % 2, (kb + j) % 2, xh, xl, weights_stationary,
                                4 * i + (2 * (base + j) + 1), 2 * i + (kb + j - 1))

            def down_unit(slot, kt, wait_lo, first, last, xh=None, xl=None):
                if last:
                    pe.wait_ge(lo_done, wait_lo + 1)
                    for m in range(2):
                        xs = slice(P * m, P * m + P)
                        for n in range(2):
                            for half in range(2):
                                at = 2048 * slot + 1024 * half + 512 * n
                                mm = passes(bank[DOWN[2 * m + n]][:, :],
                                            ((yh_[:, kt + half, xs], yl_[:, kt + half, xs]),
                                             (w_hi[:, at:at + 512], w_lo[:, at:at + 512])), False, half == 1)
                        if m == 0:
                            mm.then_inc(tile0_out, 1)
                    mm.then_inc(half_done, 2)
                    return
                for half in range(2):
                    pe.wait_ge(lo_done, wait_lo + half)
                    for m in range(2):
                        xs = slice(P * m, P * m + P)
                        for n in range(2):
                            at = 2048 * slot + 1024 * half + 512 * n
                            mm = passes(bank[DOWN[2 * m + n]][:, :],
                                        ((yh_[:, kt + half, xs], yl_[:, kt + half, xs]),
                                         (w_hi[:, at:at + 512], w_lo[:, at:at + 512])),
                                        first and half == 0, last and half == 1)
                    mm.then_inc(half_done, 1)

            def down_phase(name):
                for j in range(COUNT[name]):
                    u = UNIT0[name] + j
                    down_unit(u % 2, 2 * j, 2 * u + 1, j == 0, j == COUNT[name] - 1)

            turned = [0]

            def turn(src):
                for k in range(8):
                    n = turned[0]
                    turned[0] += 1
                    if n >= 2:
                        pe.wait_ge(tV, n - 1)
                    for m in range(2):
                        mm = pe.transpose(bank[6 + n % 2][:, P * m:P * m + P], src[:, m, P * k:P * k + P], ident)
                    mm.then_inc(tT, 1)

            def turn_mk(n):
                pe.wait_ge(mkn_ready, n)
                pe.wait_ge(tV, turned[0])
                for hd in range(4):
                    for m in range(2):
                        mm = pe.transpose(bank[6 + hd // 2][:, SEQ * (hd % 2) + P * m:SEQ * (hd % 2) + P * m + P],
                                          MKN[:, m, P * hd:P * hd + P], ident)
                mm.then_inc(mk_t, 1)

            def st_turn_qk(g):
                kind, hd = HEADS[g]
                if kind == "G":
                    return
                if hd == 0:
                    pe.wait_ge(qk_ready, 1 + "AXCY".index(kind))
                if g in (0, 12):
                    pe.wait_ge(mk_ready, 1 if g == 0 else 2)
                if g >= 1:
                    pe.wait_ge(a_qk, g)
                q, k = {"A": (eQ, eK), "X": (eXQ, None), "C": (oQ, oK), "Y": (oXQ, None)}[kind]
                cs = slice(P * hd, P * hd + P)
                for n, src in enumerate((q, k)):
                    if src is not None:
                        for m in range(2):
                            at = SEQ * n + P * m
                            mm = pe.transpose(bank[TRB][:, at:at + P], src[:, m, cs], ident)
                mm.then_inc(a_tr, 1)

            def st_scores(g):
                kind, hd = HEADS[g]
                pr = g % 2
                if kind != "G":
                    pe.wait_ge(a_qk, g + 1)
                if kind == "G" and hd == 0:
                    pe.wait_ge(evacuated, BANK0["xq0" if g < 32 else "xq1"] + 4)
                if kind in "XY" and hd == 0:
                    pe.wait_ge(mk_ready, 1 if kind == "X" else 2)
                if kind == "C" and hd == 0:
                    pe.wait_ge(cum_ready, 1)
                if kind == "A" or (kind == "X" and hd == 0):
                    if g >= 1:
                        pe.wait_ge(a_mx, g)
                else:
                    pe.wait_ge(a_mx, g - 1)
                    pe.wait_ge(a_ex, g - 1)
                q, k = qk[pr][:, 0:SEQ], qk[pr][:, SEQ:512]
                if kind == "A":
                    for c in range(2):
                        ps = slice(64 * c, 64 * c + 64)
                        pe.matmul(bank[SC[c]][:, 0:P], q[ps, 0:P], k[ps, 0:P], start=True, stop=True)
                        mm = pe.matmul(bank[SC[c]][:, P:384], q[ps, P:SEQ], k[ps, :], start=True, stop=True)
                elif kind == "C":
                    b = bank[SC[pr]]
                    pick = ident[0:12, hd:hd + 1].to_broadcast([12, P])
                    pe.matmul(b[:, 0:P], q[:, 0:P], k[:, 0:P], start=True, stop=False)
                    pe.matmul(b[:, 0:P], pick, cumT[:, 0:P], start=False, stop=True)
                    pe.matmul(b[:, P:384], q[:, P:SEQ], k[:, :], start=True, stop=False)
                    mm = pe.matmul(b[:, P:384], pick, cumT[:, :], start=False, stop=True)
                elif kind in "XY":
                    for m in range(2):
                        mm = pe.matmul(bank[SC[pr]][:, SEQ * m:SEQ * m + SEQ], q[:, P * m:P * m + P],
                                       MKT[:, hd, :], start=True, stop=True)
                else:
                    for m in range(2):
                        for j in range(2):
                            mm = pe.matmul(bank[SC[pr]][:, SEQ * m:SEQ * m + SEQ],
                                           XQT[:, 2 * hd + j, P * m:P * m + P], KT2[:, 2 * hd + j, :],
                                           start=(j == 0), stop=(j == 1))
                mm.then_inc(a_sc, 1)

            def st_turn_p(g):
                kind, _ = HEADS[g]
                s = Sb[g % 2]
                if kind == "A":
                    pe.wait_ge(a_pn, g + 1)
                else:
                    pe.wait_ge(a_ex, g + 1)
                if g >= 1:
                    pe.wait_ge(a_pe, g)
                if kind in "AC":
                    blocks = [(0, 0), (P, P), (2 * P, 2 * P)]
                else:
                    blocks = [(SEQ * m + P * k, SEQ * k + P * m) for m in range(2) for k in range(2)]
                for src, dst in blocks:
                    mm = pe.transpose(bank[PTB][:, dst:dst + P], s[:, src:src + P], ident)
                mm.then_inc(a_pt, 1)

            def st_values(g):
                kind, hd = HEADS[g]
                p = pT[g % 2]
                pe.wait_ge(a_pe, g + 1)
                if g >= 1:
                    pe.wait_ge(a_yn, g)
                v, w = {"A": (eV, P), "X": (MV, P), "C": (oV, P), "Y": (MV, P), "G": (V2, SEQ)}[kind]
                cs = slice(w * hd, w * hd + w)
                o = bank[OB]
                if kind in "AC":
                    if hd % 2 == 0:
                        pe.wait_ge(evacuated, v_unit(kind, hd))
                    pe.matmul(o[:, 0:w], p[:, 0:P], v[:, 0, cs], start=True, stop=True)
                    pe.matmul(o[:, w:2 * w], p[:, P:2 * P], v[:, 0, cs], start=True, stop=False)
                    mm = pe.matmul(o[:, w:2 * w], p[:, 2 * P:384], v[:, 1, cs], start=False, stop=True)
                else:
                    for m in range(2):
                        for k in range(2):
                            mm = pe.matmul(o[:, w * m:w * m + w], p[:, SEQ * k + P * m:SEQ * k + P * m + P],
                                           v[:, k, cs], start=(k == 0), stop=(k == 1))
                mm.then_inc(a_pv, 1)

            def st_turn_y(g):
                kind, _ = HEADS[g]
                pe.wait_ge(a_yn, g + 1)
                if g >= 1:
                    pe.wait_ge(a_yl, g)
                w = SEQ if kind == "G" else P
                for j in range(w // P):
                    for m in range(2):
                        mm = pe.transpose(bank[YTB][:, SEQ * j + P * m:SEQ * j + P * m + P],
                                          ys[g % 2][:, w * m + P * j:w * m + P * j + P], ident)
                mm.then_inc(a_yt, 1)

            def attention(name):
                lo, hi = PASS[name]
                for s in range(lo, hi + LAG):
                    for lag, stage in ((5, st_turn_y), (3, st_turn_p), (1, st_scores), (4, st_values), (0, st_turn_qk)):
                        if lo <= s - lag < hi:
                            stage(s - lag)
                    phase, before, count = BESIDE[name]
                    j = before + s - lo
                    if s - lo < count:
                        u, kb = UNIT0[phase] + j, BANK0[phase] + j
                        k8_unit(u % 2, kb % 2, uh, ul, False, 2 * u + 1, kb - 1)

            def ffn(name, layer):
                base, kb = UNIT0[name], BANK0[name]

                def gate_up(off, par, lo_w, ev_w, fresh=None):
                    k8_unit((base + off) % 2, (kb + par) % 2, uh, ul, True, lo_w, ev_w, fresh)
                    slot, bk = (base + off + 1) % 2, 6 + par
                    for half in range(2):
                        pe.wait_ge(lo_done, lo_w + 2 + half)
                        for m in range(2):
                            for k in range(4 * half, 4 * half + 4):
                                a = 2048 * slot + SEQ * k + P * m
                                mm = passes(bank[bk][:, SEQ * m:SEQ * m + SEQ],
                                            ((w_hi[:, a:a + P], w_lo[:, a:a + P]), (uh[:, k, :], ul[:, k, :])),
                                            half == 0 and m == 0 and k == 0, k == 7)
                        mm.then_inc(half_done, 1)

                hs = layer * FFN_STEPS
                gate_up(0, 0, 2 * base + 1, kb - 1, 48 + 16 * layer)
                pe.wait_ge(zrow_done, 1)
                for b in DOWN:
                    pe.matmul(bank[b][:, :], zrow[0:1, 0:P], zrow[0:1, 0:512], start=True, stop=False,
                              skip_group_check=True)
                with pe.Fori(0, (FFN_STEPS - 1) // 2) as i:
                    for j in range(2):
                        s = 1 + j
                        gate_up(2 + 3 * j, s % 2, 12 * i + (2 * (base + 2 + 3 * j) + 1), 2 * i + (kb + s - 1))
                        pe.wait_ge(h_split, 2 * i + (hs + s))
                        u = base + 4 + 3 * j
                        down_unit(u % 2, 2 * ((s - 1) % 2), 12 * i + (2 * u + 1), False, False)
                pe.wait_ge(h_split, hs + FFN_STEPS)
                u = base + 3 * FFN_STEPS - 1
                down_unit(u % 2, 2 * ((FFN_STEPS - 1) % 2), 2 * u + 1, False, True)

            pe.wait_ge(cst_in, 16)
            pe.wait_ge(rows_in, 16 * 10)
            pe.transpose(bank[5][:, 0:G1_N], rows[0:G1_N, 0:P], ident[0:G1_N, 0:G1_N]).then_inc(gains_t, 1)
            pe.wait_ge(nrm_ready, 2)
            turn(nrm)
            pe.wait_ge(rows2_in, 16 * 17)
            pe.transpose(bank[4][:, 0:G2_N], rows[0:G2_N, P:2 * P], ident[0:G2_N, 0:G2_N])
            pe.transpose(bank[4][:, G2_N:G2_N + G3_N], rows[0:G3_N, 2 * P:384], ident[0:G3_N, 0:G3_N])\
                .then_inc(gains_t, 1)
            pe.wait_ge(memG_ready, 8)
            k8_phase("e_kv", yh_, yl_, False, 2)
            pe.wait_ge(nrm_ready, 4)
            turn(nrm)
            k8_phase("e_kv", yh_, yl_, False, 2, 2)
            k8_phase("e_conv", uh, ul, True, fresh=8)
            turn_mk(1)
            k8_phase("e_nat", uh, ul, False, BESIDE["e"][1])
            attention("e")
            pe.wait_ge(a_yl, 12)
            pe.wait_ge(conv_lo, 1)
            down_phase("e_out")
            pe.wait_ge(memG_ready, 16)
            k8_phase("o_kv", yh_, yl_, False, 2)
            pe.wait_ge(nrm_ready, 6)
            turn(nrm)
            k8_phase("o_kv", yh_, yl_, False, 2, 2)
            k8_phase("o_nat", uh, ul, False, 6, fresh=16)
            turn_mk(2)
            k8_phase("o_nat", uh, ul, False, 4, 6)
            pe.wait_ge(cf_split, 2)
            pe.wait_ge(mk_ready, 2)
            for m in range(2):
                for k in range(8):
                    xs = slice(P * m, P * m + P)
                    mm = passes(bank[7][:, 12 * m:12 * m + 12],
                                ((uh[:, k, xs], ul[:, k, xs]), (cf_hi[:, 12 * k:12 * k + 12], cf_lo[:, 12 * k:12 * k + 12])),
                                m == 0 and k == 0, k == 7)
            mm.then_inc(cf_mm, 1)
            k8_phase("o_nat", uh, ul, False, 4, 10)
            pe.wait_ge(cf_dve, 3)
            tri = cst[:, C_TRI:C_TRI + P]
            pe.matmul(bank[7][0:12, 0:P], cfl[:, 0:12], tri, start=True, stop=True)
            pe.matmul(bank[7][0:12, P:SEQ], cfl[:, 0:12], ones[:, :], start=True, stop=False)
            pe.matmul(bank[7][0:12, P:SEQ], cfl[:, 12:24], tri, start=False, stop=True).then_inc(cum_mm, 1)
            attention("o")
            pe.wait_ge(a_yl, 28)
            down_phase("o_out")
            pe.wait_ge(h_ready, 2)
            turn(hv)
            k8_phase("ab_t", uh, ul, True, 2, fresh=24)
            pe.wait_ge(nrm_ready, 8)
            turn(nrm)
            k8_phase("ab_t", uh, ul, True, 6, 2)
            k8_phase("ab_nat", uh, ul, False)
            pe.wait_ge(tL, 32)
            k8_phase("xk0", yh_[:, 8:16, :], yl_[:, 8:16, :], True)
            k8_phase("xv0", yh_[:, 8:16, :], yl_[:, 8:16, :], False)
            pe.wait_ge(up_ready, 1)
            pe.wait_ge(evacuated, BANK0["xv0"] + 4)
            pe_tap = [0]

            def conv_taps(n):
                for _ in range(min(n, CV_PE - pe_tap[0])):
                    i = pe_tap[0]
                    pe_tap[0] += 1
                    pe.wait_ge(diag_ready, i + 1)
                    k = CV_K - CV_PE + i
                    for f in range(4):
                        mm = pe.matmul(bank[f // 2][:, SEQ * (f % 2):SEQ * (f % 2) + SEQ],
                                       DIAG[i % 2][:, P * f:P * f + P], UP[:, f, k:k + SEQ],
                                       start=(i == 0 and f % 2 == 0), stop=(i == CV_PE - 1), skip_group_check=True)
                    mm.then_inc(diag_used, 1)

            conv_taps(PE_FIRST)
            pe.wait_ge(hg_k, 1)
            for m in range(2):
                for f in range(4):
                    mm = pe.transpose(bank[2 + m][:, P * f:P * f + P], LF[:, f, P * m:P * m + P], ident)
            mm.then_inc(hg_tr, 1)
            for m in range(2):
                for f in range(4):
                    mm = pe.matmul(bank[4 + m][:, P * f:P * f + P], KT[:, f, P * m:P * m + P],
                                   HQ[:, f, P * m:P * m + P], start=True, stop=True)
            mm.then_inc(hg_st, 1)
            pe.wait_ge(hg_kn, 1)
            for n in range(N_CHUNK - 1):
                if n >= 2:
                    pe.wait_ge(hg_s, n - 1)
                m, r = n // 4, slice(32 * (n % 4), 32 * (n % 4) + 32)
                for f in range(4):
                    mm = pe.matmul(bank[6 + n % 2][:, P * f:P * f + P], KN[r, m, P * f:P * f + P],
                                   HV[r, m, P * f:P * f + P], start=True, stop=True, tile_position=(32 * (n % 4), 0))
                mm.then_inc(hg_ds, 1)
                conv_taps(1)
            conv_taps(CV_PE - pe_tap[0])
            pe.wait_ge(hg_sm, 2)
            for m in range(2):
                for f in range(4):
                    pe.matmul(bank[2 + m][:, P * f:P * f + P], STM[:, m, P * f:P * f + P], HV[:, m, P * f:P * f + P],
                              start=(f == 0), stop=False, skip_group_check=True)
                for j in range(4):
                    n = 4 * m + j
                    if n == 0:
                        continue
                    pe.wait_ge(hg_s, n)
                    for f in range(4):
                        mm = pe.matmul(bank[2 + m][32 * j:32 * j + 32, P * f:P * f + P],
                                       HQ[:, f, P * m + 32 * j:P * m + 32 * j + 32], STATE[:, n, P * f:P * f + P],
                                       start=False, stop=(j == 3), skip_group_check=True)
                mm.then_inc(hg_o, 1)
            pe.wait_ge(conv_ready, 2)
            for f in range(4):
                mm = pe.matmul(bank[4][:, 0:SEQ], ones[:, :], CA[:, f, :], start=(f == 0), stop=(f == 3))
            mm.then_inc(cv_mu, 1)
            pe.wait_ge(cv_c, 2)
            for f in range(4):
                mm = pe.matmul(bank[5][:, 0:SEQ], ones[:, :], CS[:, f, :], start=(f == 0), stop=(f == 3))
            mm.then_inc(cv_var, 1)
            pe.wait_ge(hg_y, 1)
            for f in range(4):
                for m in range(2):
                    mm = pe.transpose(bank[6 + f // 2][:, SEQ * (f % 2) + P * m:SEQ * (f % 2) + P * m + P],
                                      ON[:, m, P * f:P * f + P], ident)
            mm.then_inc(hg_yt, 1)
            pe.wait_ge(hg_yl, 1)
            pe.wait_ge(conv_lo, 2)
            down_phase("ab_out")
            for layer in range(2):
                if layer == 1:
                    k8_phase("xv1", yh_[:, 8:16, :], yl_[:, 8:16, :], False, 2)
                    pe.wait_ge(pool_in, 48)
                    pe.wait_ge(h_ready, 5)
                    for c in range(8):
                        b = bank[2 + (c // 2) % 4]
                        at = SEQ * (c % 2)
                        pe.matmul(b[:, at:at + SEQ], hv[:, 0, P * c:P * c + P], PM[:, c // 2, 0:SEQ],
                                  start=True, stop=False, skip_group_check=True)
                        mm = pe.matmul(b[:, at + P:at + SEQ], hv[:, 1, P * c:P * c + P], PM[:, c // 2, SEQ:384],
                                       start=False, stop=True, skip_group_check=True)
                        if c % 2:
                            mm.then_inc(pm_mm, 1)
                    pe.wait_ge(pm_ev, 4)
                    for m in range(2):
                        for g in range(4):
                            o = bank[DOWN[2 * m + g // 2]][:, SEQ * (g % 2):SEQ * (g % 2) + SEQ]
                            for k in range(2):
                                mm = pe.matmul(o, PT_[:, 2 * g + k, P * m:P * m + P], PW[:, 2 * g + k, :],
                                               start=(k == 0), stop=(k == 1))
                    mm.then_inc(pm_out, 1)
                    k8_phase("xv1", yh_[:, 8:16, :], yl_[:, 8:16, :], False, 2, 2)
                pe.wait_ge(nrm_ready, 10 + 6 * layer)
                turn(nrm)
                k8_phase(f"xq{layer}", uh, ul, True, fresh=40 + 16 * layer)
                attention(f"x{layer}")
                pe.wait_ge(a_yl, 32 + 4 * layer)
                down_phase(f"xo{layer}")
                if layer == 0:
                    k8_phase("xk1", yh_[:, 8:16, :], yl_[:, 8:16, :], True)
                pe.wait_ge(nrm_ready, 12 + 6 * layer)
                turn(nrm)
                ffn(f"ffn{layer}", layer)

        @block.scalar
        def _(act):
            steps = [0]

            def mark(ins):
                ins.then_inc(act_step, 1)
                steps[0] += 1

            def hi(slot, half, landed, free):
                act.wait_ge(w_landed[slot], landed)
                if free is not None:
                    act.wait_ge(half_done, free)
                at = 2048 * slot + 1024 * half
                act.activation(w_hi[:, at:at + 1024], w_raw[:, at:at + 1024], ACT.Copy).then_inc(hi_done, 1)

            def step(u, evac, kappa, i=None):
                v = u + 2
                i_land, i_half = (16 * i, 4 * i) if i is not None else (0, 0)
                live = i is not None or v < UNITS
                if live:
                    hi(v % 2, 0, i_land + 16 * (v // 2 + 1), i_half + (2 * u + 1))
                act.wait_ge(half_done, i_half + (2 * u + 2))
                if evac is not None:
                    evac(kappa % 2)
                if live:
                    hi(v % 2, 1, i_land + 16 * (v // 2 + 1), i_half + (2 * u + 2))

            def copy_out(dst, col, func=ACT.Copy):
                def go(b):
                    act.activation(dst(col), two(bank[b][:, :], SEQ), func).then_inc(evacuated, 1)
                return go

            def stream(name, skip, n, dst, func=ACT.Copy):
                base, kb = UNIT0[name] + skip, BANK0[name] + skip
                if n >= 4:
                    with act.Fori(0, n // 2) as i:
                        for j in range(2):
                            step(base + j, copy_out(dst, 2 * i + j, func), kb + j, i)
                else:
                    for j in range(n):
                        step(base + j, copy_out(dst, j, func), kb + j)

            def nat_dst(r):
                return lambda c: r[:, :, bass.ds(SEQ * c, SEQ)] if not isinstance(c, int) else r[:, :, SEQ * c:SEQ * c + SEQ]

            def t_dst(r):
                return lambda c: r[:, bass.ds(2 * c, 2), :] if not isinstance(c, int) else r[:, 2 * c:2 * c + 2, :]

            gained = [0]

            def gain_turned(g, b=None):
                for k in range(8):
                    n = gained[0]
                    gained[0] += 1
                    act.wait_ge(tT, n + 1)
                    if n >= 8:
                        act.wait_ge(tL_or_mem(n), tl_need(n))
                    act.activation(vT[:, k, :], bank[6 + n % 2][:, 0:SEQ], ACT.Identity,
                                   scale=gT[:, g + k:g + k + 1] if g is not None else 1.0,
                                   bias=gT[:, b + k:b + k + 1] if b is not None else 0.0).then_inc(tV, 1)

            def tL_or_mem(n):
                return memG_ready if n < 16 else tL

            def tl_need(n):
                return 8 if n < 16 else n - 15

            def mem_gain(k, col):
                act.activation(vT[:, k, :], memA[:, k, :], ACT.Copy, scale=gT[:, col + k:col + k + 1]).then_inc(memG_v, 1)

            def mk_gain(n, col):
                act.wait_ge(mk_t, n)
                for j in range(2):
                    ins = act.activation(MKT[:, 2 * j:2 * j + 2, :], tv(bank[6 + j][:, :]), ACT.Copy,
                                         scale=gT[:, col:col + 1])
                    mark(ins)
                act.wait_ge(act_step, steps[0])
                act.sem_inc(mk_ready, 1)

            def st_qk(g):
                kind, hd = HEADS[g]
                if kind == "G":
                    return
                act.wait_ge(a_tr, g + 1)
                if g >= 2:
                    act.wait_ge(a_sc, g - 1)
                qg = {"A": 0, "X": 1, "C": 2, "Y": 3}[kind]
                ins = act.activation(qk[g % 2][:, 0:SEQ], bank[TRB][:, 0:SEQ], ACT.Copy, scale=qs[:, qg:qg + 1])
                if kind in "AC":
                    kg = GCOL["ak" if kind == "A" else "ck"]
                    ins = act.activation(qk[g % 2][:, SEQ:512], bank[TRB][:, SEQ:512], ACT.Copy,
                                         scale=gT[:, kg:kg + 1])
                ins.then_inc(a_qk, 1)

            def st_exp(g):
                kind, _ = HEADS[g]
                p = g % 2
                act.wait_ge(a_mx, g + 1)
                if kind in "XYG":
                    if g >= 2:
                        act.wait_ge(a_pt, g - 1)
                if g >= 2:
                    act.wait_ge(a_pn, g - 1)
                if kind == "A":
                    parts = [(c, m, Sb[p][:, 384 * c + P * m:384 * c + (P if m == 0 else 384)]) for c in range(2) for m in range(2)]
                    for c, m, s in parts:
                        at = 2 * m + c
                        ins = act.activation(s, s, ACT.Exp, bias=nmax[p][:, at:at + 1], accum_out=rsum[p][:, at:at + 1])
                elif kind == "C":
                    for m in range(2):
                        s = Sb[p][:, P * m:P if m == 0 else 384]
                        ins = act.activation(s, s, ACT.Exp, bias=nmax[p][:, m:m + 1], accum_out=rsum[p][:, m:m + 1])
                else:
                    for m in range(2):
                        cs = slice(SEQ * m, SEQ * m + SEQ)
                        ins = act.activation(Sb[p][:, cs], bank[SC[p]][:, cs], ACT.Exp, bias=nmax[p][:, m:m + 1],
                                             accum_out=rsum[p][:, m:m + 1])
                ins.then_inc(a_ex, 1)

            def st_copy_p(g):
                act.wait_ge(a_pt, g + 1)
                if g >= 2:
                    act.wait_ge(a_pv, g - 1)
                n = 384 if HEADS[g][0] in "AC" else 512
                act.activation(pT[g % 2][:, 0:n], bank[PTB][:, 0:n], ACT.Copy).then_inc(a_pe, 1)

            def st_square(g):
                if HEADS[g][0] != "A":
                    return
                act.wait_ge(a_pv, g + 1)
                if g >= 2:
                    act.wait_ge(a_yn, g - 1)
                for m in range(2):
                    if m == 1 or g > 0:
                        act.wait_ge(act_step, steps[0])
                    ins = act.activation(tp[:, 256:384], bank[OB][:, P * m:P * m + P], ACT.Square,
                                         accum_out=ssq[g % 2][:, m:m + 1])
                    mark(ins)
                act.wait_ge(act_step, steps[0])
                act.sem_inc(a_sq, 1)

            def st_y_hi(g):
                kind, hd = HEADS[g]
                act.wait_ge(a_yt, g + 1)
                k0, n = {"A": (hd, 1), "X": (12 + hd, 1), "C": (hd, 1), "Y": (12 + hd, 1), "G": (2 * hd, 2)}[kind]
                act.activation(y_hi[:, SEQ * k0:SEQ * (k0 + n)], bank[YTB][:, 0:SEQ * n], ACT.Copy).then_inc(a_yh, 1)

            def attention(name):
                lo, hi_ = PASS[name]
                for s in range(lo, hi_ + LAG):
                    for lag, stage in ((5, st_y_hi), (3, st_copy_p), (4, st_square), (0, st_qk), (1, st_exp)):
                        if lo <= s - lag < hi_:
                            stage(s - lag)
                    phase, before, count = BESIDE[name]
                    j = s - lo
                    if j < count:
                        v, z, xz, heads = ((eV, eZ, eXZ, A_HEADS) if name == "e" else (oV, oZ, oXZ, C_HEADS))
                        dst, c = (xz, j - heads) if j >= heads else ((v, z)[j % 2], j // 2)
                        plain = j < heads and j % 2 == 0
                        u, kb = UNIT0[phase] + before + j, BANK0[phase] + before + j
                        step(u, copy_out(nat_dst(dst), c, ACT.Copy if plain else ACT.Silu), kb)

            def ffn(name, layer):
                base, kb = UNIT0[name], BANK0[name]

                def gate(par):
                    def go(b):
                        act.activation(SG[:, 512 * par:512 * par + 512], bank[b][:, :], ACT.Silu).then_inc(evacuated, 1)
                    return go

                def pair(i):
                    for j in range(2):
                        s = 1 + j
                        for n in range(3):
                            u = base + 2 + 3 * j + n
                            v = u + 2
                            live = not (isinstance(i, int) and v + 6 * i >= UNITS)
                            if live:
                                hi(v % 2, 0, 48 * i + 16 * (v // 2 + 1), 12 * i + (2 * u + 1))
                            act.wait_ge(half_done, 12 * i + (2 * u + 2))
                            if n == 0:
                                gate(s % 2)((kb + s) % 2)
                            if live:
                                hi(v % 2, 1, 48 * i + 16 * (v // 2 + 1), 12 * i + (2 * u + 2))

                step(base, gate(0), kb)
                step(base + 1, None, None)
                last = layer == 1
                with act.Fori(0, (FFN_STEPS - 1) // 2 - last) as i:
                    pair(i)
                if last:
                    pair((FFN_STEPS - 1) // 2 - 1)
                step(base + 3 * FFN_STEPS - 1, None, None)

            act.dma_start(cst[:, :], t["consts"]).then_inc(cst_in, 16)
            r = 0
            for name, k in G1_ROWS[:6]:
                src = t[name] if len(t[name].shape) == 1 else t[name][0]
                act.dma_start(rows[r:r + k, 0:P], src.rearrange("(k p) -> k p", p=P)).then_inc(rows_in, 16)
                r += k
            for name in ("ln_mix_g_2", "ln_mix_b_2", "ln_xa_g_2", "ln_xa_b_2"):
                act.dma_start(rows[r:r + 16, 0:P], t[name].rearrange("l (k p) -> (l k) p", p=P)).then_inc(rows_in, 16)
                r += 16
            act.wait_ge(gains_t, 1)
            act.activation(gT[:, 0:G1_N], bank[5][:, 0:G1_N], ACT.Copy).then_inc(gains_ready, 1)
            for half in range(2):
                hi(0, half, 16, None)
            for half in range(2):
                hi(1, half, 16, None)
            act.wait_ge(gains_ready, 1)
            for k in range(8):
                n = gained[0]
                gained[0] += 1
                act.wait_ge(tT, n + 1)
                act.activation(memA[:, k, :], bank[6 + n % 2][:, 0:SEQ], ACT.Copy).then_inc(tV, 1)
                act.wait_ge(tV, n + 1)
                mem_gain(k, GCOL["e_mem_norm_g"])
            act.wait_ge(gains_t, 2)
            act.activation(gT[:, G1_N:G_N], bank[4][:, 0:G_N - G1_N], ACT.Copy).then_inc(gains_ready, 1)
            act.wait_ge(gains_ready, 2)
            for n, (g, dim) in enumerate((("aq", 64), ("exq", 128), ("cq", 128), ("oxq", 128))):
                act.activation(qs[:, n:n + 1], gT[:, GCOL[g]:GCOL[g] + 1], ACT.Copy, scale=float(dim) ** -0.5)\
                    .then_inc(gains_ready, 1)
            act.wait_ge(lam_sum, 1)
            act.activation(lamw[:, 2:4], lamw[:, 0:2], ACT.Exp).then_inc(lam_exp, 1)
            stream("e_kv", 0, 2, nat_dst(MKN))
            gain_turned(GCOL["e_norm_g"])
            stream("e_kv", 2, 2, nat_dst(MV))
            for n, r in enumerate((eBH, eBC, eBB)):
                stream("e_conv", 2 * n, 2, t_dst(r))
            stream("e_conv", 6, 2, t_dst(eBZ), ACT.Silu)
            mk_gain(1, GCOL["exk"])
            stream("e_nat", 0, 4, nat_dst(eQ))
            stream("e_nat", 4, 4, nat_dst(eK))
            stream("e_nat", 8, 2, nat_dst(eXQ))
            attention("e")
            act.wait_ge(conv_ready, 1)
            act.activation(yh_[:, 8:12, :], eBC, ACT.Copy).then_inc(conv_hi, 1)
            for j in range(8):
                u = UNIT0["e_out"] + j
                step(u, None, None)
                if j >= 4:
                    if j == 4:
                        act.wait_ge(a_yl, 12)
                    for k in (2 * j - 8, 2 * j - 7):
                        mem_gain(k, GCOL["o_mem_norm_g"])
            stream("o_kv", 0, 2, nat_dst(MKN))
            for k in range(8):
                n = gained[0]
                gained[0] += 1
                act.wait_ge(tT, n + 1)
                if k == 0:
                    act.wait_ge(memG_ready, 16)
                act.activation(vT[:, k, :], bank[6 + n % 2][:, 0:SEQ], ACT.Copy,
                               scale=gT[:, GCOL["o_norm_g"] + k:GCOL["o_norm_g"] + k + 1]).then_inc(tV, 1)
            stream("o_kv", 2, 2, nat_dst(MV))
            stream("o_nat", 0, 6, nat_dst(oQ))
            mk_gain(2, GCOL["oxk"])
            stream("o_nat", 6, 4, nat_dst(oK))
            act.wait_ge(cf_dve, 1)
            act.activation(cft, cft, ACT.Exp).then_inc(cf_act, 1)
            act.wait_ge(cf_act, 1)
            act.activation(cft, cft, ACT.Ln, bias=1.0).then_inc(cf_act, 1)
            stream("o_nat", 10, 2, nat_dst(oK[:, :, 1024:]))
            stream("o_nat", 12, 2, nat_dst(oXQ))
            attention("o")
            for j in range(8):
                step(UNIT0["o_out"] + j, None, None)
            gain_turned(None)
            stream("ab_t", 0, 2, t_dst(HA))
            gain_turned(GCOL["mem_ln_g_2"], GCOL["mem_ln_b_2"])
            stream("ab_t", 2, 2, t_dst(HG), ACT.Sigmoid)
            for j in range(2):
                def forget(b, j=j):
                    act.activation(SF[:, 2 * j:2 * j + 2, :], tv(bank[b][:, :]), ACT.Sigmoid)
                    act.activation(SN[:, 2 * j:2 * j + 2, :], tv(bank[b][:, :]), ACT.Sigmoid,
                                   scale=-1.0).then_inc(evacuated, 1)
                step(UNIT0["ab_t"] + 4 + j, forget, BANK0["ab_t"] + 4 + j)
            stream("ab_t", 6, 2, t_dst(HQ))
            act.wait_ge(lb_sub, 1)
            act.activation(lbe, lbe, ACT.Exp).then_inc(lb_exp, 1)
            stream("ab_nat", 0, 2, nat_dst(HV))
            stream("ab_nat", 2, 2, nat_dst(GG), ACT.Silu)
            act.wait_ge(hg_f, 1)
            act.activation(LF, LF, ACT.Ln).then_inc(hg_ln, 1)
            stream("xk0", 0, 2, t_dst(KT2))
            act.wait_ge(hg_b, 1)
            act.activation(SF, HB, ACT.Exp)
            act.activation(KT, HB, ACT.Exp, scale=-1.0)
            act.activation(decay, HB.rearrange("p k (n c) -> p (k n) c", c=HG_CHUNK)[:, :, HG_CHUNK - 1], ACT.Exp)\
                .then_inc(hg_e, 1)
            act.wait_ge(hg_b, 2)
            act.activation(LF, LF, ACT.Exp).then_inc(hg_e, 1)
            stream("xk0", 2, 2, t_dst(KT2[:, 4:8, :]))
            stream("xv0", 0, 4, nat_dst(V2))
            act.wait_ge(tL, 32)

            def diagonals(i):
                if i >= 2:
                    act.wait_ge(diag_used, i - 1)
                for f in range(4):
                    w = GCOL["cv_w"] + 4 * (CV_K - CV_PE + i) + f
                    ins = act.activation(DIAG[i % 2][:, P * f:P * f + P], ident, ACT.Copy, scale=gT[:, w:w + 1])
                ins.then_inc(diag_ready, 1)

            for i in range(PE_FIRST):
                diagonals(i)
            act.wait_ge(hg_tr, 1)
            for m in range(2):
                ins = act.activation(KN[:, m, :], bank[2 + m][:, :], ACT.Copy)
            ins.then_inc(hg_kn, 1)
            for i in range(PE_FIRST, CV_PE):
                diagonals(i)
            for m in range(2):
                act.wait_ge(hg_o, m + 1)
                act.activation(ON[:, m, :], bank[2 + m][:, :], ACT.Copy).then_inc(hg_on, 1)
            act.wait_ge(cv_var, 1)
            act.activation(CR, bank[5][:, 0:SEQ], ACT.Sqrt, bias=epsc, scale=1.0 / B_W).then_inc(cv_sd, 1)
            for f in range(4):
                act.wait_ge(cv_x, f + 1)
                g, b = GCOL["cv_ln_g_2"] + f, GCOL["cv_ln_b_2"] + f
                act.activation(CA[:, f, :], CA[:, f, :], ACT.Silu, scale=gT[:, g:g + 1], bias=gT[:, b:b + 1])\
                    .then_inc(cv_v, 1)
            act.wait_ge(hg_yt, 1)
            for j in range(2):
                act.activation(yh_[:, 2 * j:2 * j + 2, :], tv(bank[6 + j][:, :]), ACT.Copy).then_inc(hg_yh, 1)
            for j in range(4):
                step(UNIT0["ab_out"] + j, None, None)
            for layer in range(2):
                if layer == 1:
                    stream("xv1", 0, 2, nat_dst(V2))
                    for c in range(4):
                        act.wait_ge(pm_mm, c + 1)
                        act.activation(PT_[:, 2 * c:2 * c + 2, :], tv(bank[2 + c][:, :]), ACT.Copy).then_inc(pm_ev, 1)
                    stream("xv1", 2, 2, nat_dst(V2[:, :, 512:]))
                gain_turned(GCOL["mix_g"] + 8 * layer, GCOL["mix_b"] + 8 * layer)
                base, kb = UNIT0[f"xq{layer}"], BANK0[f"xq{layer}"]
                for j in range(4):
                    def scaled(b, j=j):
                        act.activation(XQT[:, 2 * j:2 * j + 2, :], tv(bank[b][:, :]), ACT.Copy,
                                       scale=float(SEQ) ** -0.5).then_inc(evacuated, 1)
                    step(base + j, scaled, kb + j)
                act.wait_ge(h_ready, 3 + 3 * layer)
                attention(f"x{layer}")
                for j in range(4):
                    step(UNIT0[f"xo{layer}"] + j, None, None)
                if layer == 0:
                    stream("xk1", 0, 4, t_dst(KT2))
                gain_turned(GCOL["xa_g"] + 8 * layer, GCOL["xa_b"] + 8 * layer)
                ffn(f"ffn{layer}", layer)

        @block.gpsimd
        def _(pool):
            pool.memset(mhalf[:, :], -0.5).then_inc(init_done, 1)
            pool.memset(ones[:, :], 1.0).then_inc(init_done, 1)
            pool.memset(small[:, :], LN_EPS).then_inc(init_done, 1)
            pool.wait_ge(init_done, 3)

            pool.dma_start(bc[:, 0:P], t["e_a_out_norm_g"].to_broadcast([P, P])).then_inc(bc_in, 16)
            pool.dma_start(bc[:, P:P + 12], t["o_c_forget_b"].to_broadcast([P, 12])).then_inc(bc_in, 16)
            pool.dma_start(tp[:, 0:256], t["e_a_lambda"].rearrange("l a b -> l (a b)").to_broadcast([P, 256]))\
                .then_inc(lam_in, 16)

            def power(name):
                at, w = POW_AT[name]
                pool.wait_ge(pow_asked, POW_N[name])
                pool.tensor_tensor(pow_out[:, at:at + w], pow_in[:, at:at + w], mhalf[:, 0:w], ALU.pow)\
                    .then_inc(pow_done, 1)

            for name in ("mem", "x", "mk_e", "aq", "ak", "xq_e"):
                power(name)
            for g in range(A_HEADS):
                pool.wait_ge(a_sq, g + 1)
                pool.tensor_scalar(ssq[g % 2], ssq[g % 2], 1.0 / P, EPS, ALU.mult, ALU.add).then_inc(pool_step, 1)
                pool.wait_ge(pool_step, g + 1)
                pool.tensor_tensor(rout[g % 2], ssq[g % 2], mhalf[:, 0:2], ALU.pow).then_inc(a_rp, 1)
            pool.wait_ge(a_yl, 12)
            pool.dma_start(cf_raw.rearrange("p (k n) -> p k n", n=12),
                           t["o_w_in"][0][:, 6144:6156].rearrange("(k p) n -> p k n", p=P)).then_inc(cf_in, 16)
            for name in ("h1", "mk_o", "cq", "ck", "xq_o"):
                power(name)
            pool.wait_ge(a_yl, 28)
            pool.dma_start(two(att[:, 0:2 * D], D), t["mem_2"][0].rearrange("(m p) n -> p m n", p=P))\
                .then_inc(mem2_in, 16)
            power("mem2")
            pool.wait_ge(tL, 32)
            pool.dma_start(HGB, t["hg_norm_g_2"].to_broadcast([P, 512])).then_inc(hgb_in, 16)
            power("hg")

            lns = [0]

            def ln_rows(g, b):
                if lns[0]:
                    pool.wait_ge(h_ready, lns[0])
                pool.dma_start(LNG, g.to_broadcast([P, D])).then_inc(ln_in, 16)
                pool.dma_start(LNB, b.to_broadcast([P, D])).then_inc(ln_in, 16)

            def row_of(name, layer):
                return t[name][layer:layer + 1, :]

            ps = [A_HEADS]

            def natural_gain(name, n_ln):
                pool.wait_ge(ln_in, 32 * n_ln)
                for m in range(2):
                    pool.wait_ge(nrm_ready, 8 + 2 * n_ln - 1 + m)
                    pool.tensor_tensor(hv[:, m], nrm[:, m], LNG, ALU.mult).then_inc(pool_step, 1)
                    ps[0] += 1
                    pool.wait_ge(pool_step, ps[0])
                    ins = pool.tensor_tensor(hv[:, m], hv[:, m], LNB, ALU.add)
                    if m == 0:
                        ins.then_inc(pool_step, 1)
                        ps[0] += 1
                pool.wait_ge(pool_step, ps[0])
                ins.then_inc(h_ready, 1)

            pool.wait_ge(hg_yl, 1)
            ln_rows(row_of("ln_mix_g_2", 0), row_of("ln_mix_b_2", 0))
            pool.memset(zrow[:, :], 0.0).then_inc(zrow_done, 1)
            power("mix0")
            natural_gain("mix0", 1)
            lns[0] = 3
            for layer in range(2):
                if layer == 1:
                    ln_rows(row_of("ln_mix_g_2", 1), row_of("ln_mix_b_2", 1))
                    power("mix1")
                    natural_gain("mix1", 4)
                    lns[0] = 6
                ln_rows(row_of("ln_xa_g_2", layer), row_of("ln_xa_b_2", layer))
                power(f"xa{layer}")
                natural_gain(f"xa{layer}", 2 + 3 * layer)
                lns[0] = 4 + 3 * layer
                ln_rows(row_of("ln_ffn_g_2", layer), row_of("ln_ffn_b_2", layer))
                if layer == 0:
                    pool.dma_start(PM.rearrange("p g n -> p (g n)"), t["poolm"]).then_inc(pool_in, 16)
                    pool.dma_start(PW, t["pool_w_2"][0].rearrange("g (k p) n -> p (g k) n", p=P)).then_inc(pool_in, 16)
                    pool.dma_start(PSC, t["pool_scale_2"].to_broadcast([P, D])).then_inc(pool_in, 16)
                power(f"ffn{layer}")
                lns[0] = 5 + 3 * layer

        @block.vector
        def _(v):
            steps = [0]

            def mark(ins):
                ins.then_inc(dve_step, 1)
                steps[0] += 1

            def wait_own():
                v.wait_ge(dve_step, steps[0])

            def done(ins_sem):
                wait_own()
                v.sem_inc(ins_sem, 1)

            def lo(slot, half, ready):
                v.wait_ge(hi_done, ready)
                at = 2048 * slot + 1024 * half
                v.tensor_tensor(w_lo[:, at:at + 1024], w_raw[:, at:at + 1024],
                                w_hi[:, at:at + 1024].bitcast(F32), ALU.subtract).then_inc(lo_done, 1)

            def stream(name, skip=0, n=None):
                base = UNIT0[name] + skip
                n = COUNT[name] - skip if n is None else n
                if n >= 4 and n % 2 == 0 and base + n + 2 <= UNITS:
                    with v.Fori(0, n // 2) as i:
                        for j in range(2):
                            for half in range(2):
                                lo((base + j) % 2, half, 4 * i + (2 * (base + j + 2) + 1 + half))
                else:
                    for j in range(n):
                        for half in range(2):
                            if base + j + 2 < UNITS:
                                lo((base + j) % 2, half, 2 * (base + j + 2) + 1 + half)

            def ask(name):
                done(pow_asked)

            def tile_stats(src, m):
                for j in range(2):
                    mark(v.bn_stats(bn6[:, 12 * m + 6 * j:12 * m + 6 * j + 6], src[:, m, 512 * j:512 * j + 512]))

            def row_stats(src, name, eps, rms, started=False):
                at, _ = POW_AT[name]
                if not started:
                    for m in range(2):
                        tile_stats(src, m)
                wait_own()
                for m in range(2):
                    mark(v.bn_aggr(mv[:, m, :], bn6[:, 12 * m:12 * m + 12]))
                wait_own()
                o = pow_in[:, at:at + 2]
                if rms:
                    mark(v.tensor_tensor(o, mv[:, :, 0], mv[:, :, 0], ALU.mult))
                    wait_own()
                    mark(v.scalar_tensor_tensor(o, o, float(eps), mv[:, :, 1], ALU.add, ALU.add))
                else:
                    mark(v.tensor_scalar(o, mv[:, :, 1], float(eps), None, ALU.add))
                ask(name)

            def normalise(src, name, rms):
                at, _ = POW_AT[name]
                v.wait_ge(pow_done, POW_N[name])
                for m in range(2):
                    r = pow_out[:, at + m:at + m + 1]
                    if rms:
                        v.tensor_scalar(nrm[:, m], src[:, m], r, None, ALU.mult).then_inc(nrm_ready, 1)
                    else:
                        v.tensor_scalar(nrm[:, m], src[:, m], mv[:, m, 0:1], r, ALU.subtract, ALU.mult)\
                            .then_inc(nrm_ready, 1)

            def head_norm(src, sq, heads, dim, name):
                at, w = POW_AT[name]
                q = sq[:, 0:2 * heads * dim].rearrange("p (m w) -> p m w", m=2)
                mark(v.tensor_tensor(q, src, src, ALU.mult))
                wait_own()
                mark(v.tensor_reduce(pow_in[:, at:at + w], sq[:, 0:2 * heads * dim].rearrange("p (a b) -> p a b", b=dim),
                                     AX.X, ALU.add))
                wait_own()
                mark(v.tensor_scalar(pow_in[:, at:at + w], pow_in[:, at:at + w], 1.0 / dim, EPS, ALU.mult, ALU.add))
                ask(name)

            def head_scale(src_flat, heads, dim, name):
                at, w = POW_AT[name]
                v.wait_ge(pow_done, POW_N[name])
                s = src_flat.rearrange("p (a b) -> p a b", b=dim)
                r = pow_out[:, at:at + w].rearrange("p (a b) -> p a b", b=1).to_broadcast([P, w, dim])
                mark(v.tensor_tensor(s, s, r, ALU.mult))

            def split_turned(dh, dl, k0=0):
                for k in range(8):
                    v.wait_ge(tV, vt_count[0] + 1)
                    vt_count[0] += 1
                    mark(v.tensor_copy(dh[:, k0 + k, :], vT[:, k, :]))
                    wait_own()
                    v.tensor_tensor(dl[:, k0 + k, :], vT[:, k, :], dh[:, k0 + k, :].bitcast(F32), ALU.subtract)\
                        .then_inc(tL, 1)

            vt_count = [8]

            def split_mem(k, n):
                v.wait_ge(memG_v, n + 1)
                mark(v.tensor_copy(yh_[:, k, :], vT[:, k, :]))
                wait_own()
                v.tensor_tensor(yl_[:, k, :], vT[:, k, :], yh_[:, k, :].bitcast(F32), ALU.subtract)\
                    .then_inc(memG_ready, 1)

            outputs = ["e_out", "o_out", "ab_out", "xo0", "ffn0", "xo1", "ffn1"]

            def residual(name, alpha):
                for m in range(2):
                    if m == 0:
                        v.wait_ge(tile0_out, outputs.index(name) + 1)
                    else:
                        v.wait_ge(half_done, unit_end(name))
                    for n in range(2):
                        hs = hv[:, m, 512 * n:512 * n + 512]
                        mark(v.scalar_tensor_tensor(hs, hs, float(alpha), bank[DOWN[2 * m + n]][:, :], ALU.mult, ALU.add))
                    wait_own()
                    if name != "o_out":
                        tile_stats(hv, m)

            def st_max(g):
                kind, hd = HEADS[g]
                p = g % 2
                v.wait_ge(a_sc, g + 1)
                if g >= 2:
                    if kind in "AC":
                        v.wait_ge(a_pt, g - 1)
                    v.wait_ge(a_ex, g - 1)
                if kind == "A":
                    slope = 2.0 ** (-8.0 * (hd + 1) / A_HEADS)
                    for c in range(2):
                        mark(v.scalar_tensor_tensor(Sb[p][:, 384 * c:384 * c + 384], cst[:, C_DIST:C_DIST + 384],
                                                    slope, bank[SC[c]][:, 0:384], ALU.mult, ALU.add))
                    wait_own()
                    s = Sb[p].rearrange("p (c n) -> p c n", n=384)
                    mark(v.tensor_reduce(nmax[p][:, 0:2], s[:, :, 0:P], AX.X, ALU.max, negate=True))
                    ins = v.tensor_reduce(nmax[p][:, 2:4], s[:, :, P:384], AX.X, ALU.max, negate=True)
                elif kind == "C":
                    mark(v.tensor_tensor(Sb[p][:, 0:384], bank[SC[p]][:, 0:384], cst[:, C_MASK:C_MASK + 384], ALU.add))
                    wait_own()
                    mark(v.tensor_reduce(nmax[p][:, 0:1], Sb[p][:, 0:P], AX.X, ALU.max, negate=True))
                    ins = v.tensor_reduce(nmax[p][:, 1:2], Sb[p][:, P:384], AX.X, ALU.max, negate=True)
                else:
                    ins = v.tensor_reduce(nmax[p][:, 0:2], bank[SC[p]][:, :].rearrange("p (m n) -> p m n", m=2),
                                          AX.X, ALU.max, negate=True)
                return ins

            def max_stage(g):
                kind, hd = HEADS[g]
                p = g % 2
                st_max(g).then_inc(a_mx, 1)

            def st_combine(g):
                p = g % 2
                v.wait_ge(a_ex, g + 1)
                if HEADS[g][0] != "A":
                    v.reciprocal(rinv[g % 4][:, 0:2], rsum[p][:, 0:2]).then_inc(a_pn, 1)
                    return
                rl = rinv[g % 4]
                mark(v.reciprocal(rl, rsum[p]))
                wait_own()
                mark(v.tensor_scalar(plam[p], rl.rearrange("p (m c) -> p m c", c=2)[:, :, 1], nlam, None, ALU.mult))
                wait_own()
                for m in range(2):
                    a = slice(0, P) if m == 0 else slice(P, 384)
                    b = slice(384, 512) if m == 0 else slice(512, 768)
                    mark(v.tensor_scalar(Sb[p][:, b], Sb[p][:, b], plam[p][:, m:m + 1], None, ALU.mult))
                wait_own()
                for m in range(2):
                    a = slice(0, P) if m == 0 else slice(P, 384)
                    b = slice(384, 512) if m == 0 else slice(512, 768)
                    ins = v.scalar_tensor_tensor(Sb[p][:, a], Sb[p][:, a], rl[:, 2 * m:2 * m + 1], Sb[p][:, b],
                                                 ALU.mult, ALU.add)
                ins.then_inc(a_pn, 1)

            def st_y(g):
                kind, hd = HEADS[g]
                p = g % 2
                v.wait_ge(a_pv, g + 1)
                if g >= 2:
                    v.wait_ge(a_yt, g - 1)
                w = SEQ if kind == "G" else P
                cs = slice(P * hd, P * hd + P)
                if kind != "G":
                    v.wait_ge(evacuated, z_unit(kind, hd))
                if kind == "A":
                    og = bc[:, 0:P].rearrange("p (a b) -> p a b", a=1).to_broadcast([P, 2, P])
                    mark(v.scalar_tensor_tensor(eZ[:, :, cs], eZ[:, :, cs], 1.0 - LAM_INIT, og, ALU.mult, ALU.mult))
                    wait_own()
                    v.wait_ge(a_rp, g + 1)
                    r, gate = rout[p], eZ
                else:
                    v.wait_ge(a_pn, g + 1)
                    r, gate = rinv[g % 4], {"X": eXZ, "C": oZ, "Y": oXZ, "G": None}[kind]
                for m in range(2):
                    o = bank[OB][:, w * m:w * m + w]
                    y = ys[p][:, w * m:w * m + w]
                    if gate is None:
                        ins = v.tensor_scalar(y, o, r[:, m:m + 1], None, ALU.mult)
                    else:
                        ins = v.scalar_tensor_tensor(y, o, r[:, m:m + 1], gate[:, m, cs], ALU.mult, ALU.mult)
                ins.then_inc(a_yn, 1)

            def st_y_lo(g):
                kind, hd = HEADS[g]
                v.wait_ge(a_yh, g + 1)
                k0, n = {"A": (hd, 1), "X": (12 + hd, 1), "C": (hd, 1), "Y": (12 + hd, 1), "G": (2 * hd, 2)}[kind]
                s = slice(SEQ * k0, SEQ * (k0 + n))
                v.tensor_tensor(y_lo[:, s], bank[YTB][:, 0:SEQ * n], y_hi[:, s].bitcast(F32), ALU.subtract)\
                    .then_inc(a_yl, 1)

            def gated_conv(part):
                cw, cb = GCOL["e_b_conv_w"], GCOL["e_b_conv_b"]
                if part == 0:
                    v.wait_ge(evacuated, BANK0["e_conv"] + 8)
                    mark(v.tensor_tensor(eBH, eBH, eBC, ALU.mult))
                    wait_own()
                    for f in range(4):
                        mark(v.tensor_scalar(eBC[:, f, :], eBH[:, f, :], gT[:, cw + 8 + f:cw + 9 + f],
                                             gT[:, cb + f:cb + f + 1], ALU.mult, ALU.add))
                elif part < 3:
                    tap = 2 - part
                    sh = CONV_W - 1 - tap
                    wait_own()
                    for f in range(4):
                        mark(v.scalar_tensor_tensor(eBC[:, f, sh:SEQ], eBH[:, f, 0:SEQ - sh],
                                                    gT[:, cw + 4 * tap + f:cw + 4 * tap + f + 1], eBC[:, f, sh:SEQ],
                                                    ALU.mult, ALU.add))
                else:
                    mark(v.tensor_tensor(eBB, eBB, eBZ, ALU.mult))
                    wait_own()
                    mark(v.tensor_tensor(eBC, eBC, eBB, ALU.mult))
                    done(conv_ready)

            def attention(name):
                lo_, hi_ = PASS[name]
                for s in range(lo_, hi_ + LAG):
                    for lag, stage in ((5, st_y_lo), (2, st_combine), (1, max_stage), (4, st_y)):
                        if lo_ <= s - lag < hi_:
                            stage(s - lag)
                    phase, before, count = BESIDE[name]
                    if name == "e" and count <= s - lo_ < count + 4:
                        gated_conv(s - lo_ - count)
                    if s - lo_ < count:
                        stream(phase, before + s - lo_, 1)
                    if s in (lo_, lo_ + 2) and count:
                        src, flat, sq, what = ((eXQ, nat[:, 8192:9216], nat[:, 9216:10240], "xq_e") if name == "e" else
                                               (oXQ, nat[:, 12288:13312], nat[:, 13312:14336], "xq_o"))
                        if s == lo_:
                            v.wait_ge(evacuated, BANK0[phase] + before)
                            head_norm(src, sq, X_HEADS, P, what)
                        else:
                            head_scale(flat, X_HEADS, P, what)
                            done(qk_ready)

            def ffn(name, layer):
                base = UNIT0[name]
                hs = layer * FFN_STEPS

                def hidden(par, gate, up):
                    v.wait_ge(evacuated, gate)
                    v.wait_ge(half_done, up)
                    f = HF[:, 512 * par:512 * par + 512]
                    v.tensor_tensor(f, SG[:, 512 * par:512 * par + 512], bank[6 + par][:, :], ALU.mult).then_inc(ff_a, 1)
                    return f

                def pair(i):
                    for j in range(2):
                        s = 1 + j
                        u = base + 2 + 3 * j
                        for n in range(2):
                            stream_one(u + n, i)
                        hidden(s % 2, 2 * i + (kb + s + 1), 12 * i + (2 * u + 4))
                        finish_hidden(s % 2, 2 * i + (hs + s + 1))
                        stream_one(u + 2, i)

                kb = BANK0[name]
                stream_one(base, 0)
                stream_one(base + 1, 0)
                hidden(0, kb + 1, 2 * base + 4)
                finish_hidden(0, hs + 1)
                last = layer == 1
                with v.Fori(0, (FFN_STEPS - 1) // 2 - last) as i:
                    pair(i)
                if last:
                    pair((FFN_STEPS - 1) // 2 - 1)
                stream_one(base + 3 * FFN_STEPS - 1, 0)

            def stream_one(u, i):
                x = u + 2
                if isinstance(i, int) and x + 6 * i >= UNITS:
                    return
                for half in range(2):
                    lo(x % 2, half, 12 * i + (2 * x + 1 + half))

            def finish_hidden(par, count):
                f = HF[:, 512 * par:512 * par + 512]
                s = slice(512 * par, 512 * par + 512)
                v.wait_ge(ff_a, count)
                v.tensor_copy(y_hi[:, s], f).then_inc(ff_b, 1)
                v.wait_ge(ff_b, count)
                v.tensor_tensor(y_lo[:, s], f, y_hi[:, s].bitcast(F32), ALU.subtract).then_inc(h_split, 1)

            v.wait_ge(init_done, 3)
            v.wait_ge(mem_in, 16)
            row_stats(nrm, "mem", EPS, True)
            normalise(nrm, "mem", True)
            for slot in range(2):
                for half in range(2):
                    lo(slot, half, 2 * slot + half + 1)
            for k in range(8):
                split_mem(k, k)
            v.wait_ge(x_in, 16)
            row_stats(hv, "x", EPS, True)
            normalise(hv, "x", True)
            v.wait_ge(lam_in, 16)
            lm = tp[:, 0:256].rearrange("p (a b) -> p a b", b=64)
            mark(v.tensor_tensor(tp[:, 256:320], lm[:, 0], lm[:, 1], ALU.mult))
            mark(v.tensor_tensor(tp[:, 320:384], lm[:, 2], lm[:, 3], ALU.mult))
            wait_own()
            mark(v.tensor_reduce(lamw[:, 0:2], tp[:, 256:384].rearrange("p (a b) -> p a b", b=64), AX.X, ALU.add))
            done(lam_sum)
            v.wait_ge(lam_exp, 1)
            mark(v.tensor_tensor(nlam, lamw[:, 3:4], lamw[:, 2:3], ALU.subtract))
            wait_own()
            mark(v.tensor_scalar(nlam, nlam, -LAM_INIT, None, ALU.add))
            stream("e_kv", 0, 2)
            split_turned(uh, ul)
            stream("e_kv", 2, 2)
            v.wait_ge(evacuated, 2)
            head_norm(MKN, msq, 4, P, "mk_e")
            head_scale(nat[:, 6144:7168], 4, P, "mk_e")
            done(mkn_ready)
            stream("e_conv")
            stream("e_nat", 0, 4)
            stream("e_nat", 4, 2)
            kb = BANK0["e_nat"]
            v.wait_ge(evacuated, kb + 4)
            head_norm(eQ, att[:, 0:2048], 16, 64, "aq")
            stream("e_nat", 6, 2)
            head_scale(nat[:, 0:2048], 16, 64, "aq")
            v.wait_ge(evacuated, kb + 8)
            head_norm(eK, att[:, 0:2048], 16, 64, "ak")
            stream("e_nat", 8, 2)
            head_scale(nat[:, 2048:4096], 16, 64, "ak")
            done(qk_ready)
            v.wait_ge(bc_in, 32)
            attention("e")
            v.wait_ge(conv_hi, 1)
            v.tensor_tensor(yl_[:, 8:12, :], eBC, yh_[:, 8:12, :].bitcast(F32), ALU.subtract).then_inc(conv_lo, 1)
            for j in range(8):
                stream("e_out", j, 1)
                if j >= 4:
                    for k in (2 * j - 8, 2 * j - 7):
                        split_mem(k, 8 + k)
            residual("e_out", 1.0)
            v.sem_inc(h_ready, 1)
            row_stats(hv, "h1", EPS, True, True)
            stream("o_kv", 0, 1)
            normalise(hv, "h1", True)
            stream("o_kv", 1, 1)
            split_turned(uh, ul)
            stream("o_kv", 2, 2)
            v.wait_ge(evacuated, BANK0["o_kv"] + 2)
            head_norm(MKN, msq, 4, P, "mk_o")
            head_scale(nat[:, 6144:7168], 4, P, "mk_o")
            done(mkn_ready)
            v.wait_ge(cf_in, 16)
            mark(v.tensor_copy(cf_hi[:, :], cf_raw))
            done(cf_split)
            v.tensor_tensor(cf_lo[:, :], cf_raw, cf_hi[:, :].bitcast(F32), ALU.subtract).then_inc(cf_split, 1)
            stream("o_nat", 0, 6)
            kb = BANK0["o_nat"]
            v.wait_ge(evacuated, kb + 6)
            head_norm(oQ, att[:, 0:3072], 12, P, "cq")
            stream("o_nat", 6, 2)
            head_scale(nat[:, 0:3072], 12, P, "cq")
            stream("o_nat", 8, 2)
            v.wait_ge(cf_mm, 1)
            fb = bc[:, P:P + 12].rearrange("p (a b) -> p a b", a=1).to_broadcast([P, 2, 12])
            c3 = cfl.rearrange("p (m n) -> p m n", m=2)
            mark(v.tensor_tensor(c3, bank[7][:, 0:24].rearrange("p (m n) -> p m n", m=2), fb, ALU.add))
            wait_own()
            mark(v.tensor_scalar(cft, cfl, -1.0, None, ALU.mult))
            wait_own()
            mark(v.tensor_tensor(cft, cft, cfl, ALU.min))
            done(cf_dve)
            mark(v.tensor_scalar(cfl, cfl, 0.0, None, ALU.min))
            done(cf_dve)
            v.wait_ge(cf_act, 2)
            wait_own()
            v.tensor_tensor(cfl, cft, cfl, ALU.subtract).then_inc(cf_dve, 1)
            stream("o_nat", 10, 2)
            v.wait_ge(evacuated, kb + 12)
            head_norm(oK, att[:, 0:3072], 12, P, "ck")
            stream("o_nat", 12, 2)
            head_scale(nat[:, 3072:6144], 12, P, "ck")
            done(qk_ready)
            v.wait_ge(cum_mm, 1)
            v.tensor_copy(cumT, bank[7][0:12, 0:SEQ]).then_inc(cum_ready, 1)
            attention("o")
            stream("o_out", 0, 2)
            v.wait_ge(mem2_in, 16)
            row_stats(nrm, "mem2", LN_EPS, False)
            stream("o_out", 2, 2)
            normalise(nrm, "mem2", False)
            stream("o_out", 4, 4)
            residual("o_out", 1.0)
            v.sem_inc(h_ready, 1)
            split_turned(uh, ul)
            stream("ab_t", 0, 2)
            split_turned(yh_, yl_, 8)
            lp = gT[:, GCOL["lb_param_2"]:GCOL["lb_param_2"] + 12].rearrange("p (w k) -> p k w", k=4)
            le = lbe.rearrange("p (w k) -> p k w", k=4)
            mark(v.tensor_reduce(lbm, lp, AX.X, ALU.max))
            wait_own()
            mark(v.tensor_tensor(lbe.rearrange("p (w k) -> p w k", k=4), gT[:, GCOL["lb_param_2"]:GCOL["lb_param_2"] + 12]
                                 .rearrange("p (w k) -> p w k", k=4),
                                 lbm.rearrange("p (w k) -> p w k", w=1).to_broadcast([P, 3, 4]), ALU.subtract))
            done(lb_sub)
            mark(v.memset(UP, 0.0))
            stream("ab_t", 2, 2)
            kb = BANK0["ab_t"]
            v.wait_ge(evacuated, kb + 4)
            wait_own()
            mark(v.tensor_tensor(UP[:, :, 30:], HA, HG, ALU.mult))
            done(up_ready)
            tap = [0]

            def taps(n):
                for _ in range(n):
                    k = tap[0]
                    tap[0] += 1
                    if k >= CV_K - CV_PE:
                        return
                    wait_own()
                    for f in range(4):
                        wcol = GCOL["cv_w"] + 4 * k + f
                        ws = gT[:, wcol:wcol + 1]
                        if k == 0:
                            b = GCOL["cv_b_2"] + f
                            mark(v.tensor_scalar(CA[:, f, :], UP[:, f, 0:SEQ], ws, gT[:, b:b + 1], ALU.mult, ALU.add))
                        else:
                            mark(v.scalar_tensor_tensor(CA[:, f, :], UP[:, f, k:k + SEQ], ws, CA[:, f, :],
                                                        ALU.mult, ALU.add))

            for j in range(4):
                stream("ab_t", 4 + j, 1)
                taps(2)
            v.wait_ge(lb_exp, 1)
            mark(v.tensor_reduce(lbs, le, AX.X, ALU.add))
            wait_own()
            mark(v.reciprocal(lbs, lbs))
            wait_own()
            mark(v.tensor_tensor(lb, lbs, lbe[:, 0:4], ALU.mult))
            wait_own()
            mark(v.tensor_scalar(oml, lb, -1.0, 1.0, ALU.mult, ALU.add))
            stream("ab_nat", 0, 1)
            wait_own()
            v.wait_ge(evacuated, kb + 6)
            for f in range(4):
                mark(v.tensor_scalar(LF[:, f, :], SF[:, f, :], oml[:, f:f + 1], lb[:, f:f + 1], ALU.mult, ALU.add))
            done(hg_f)
            stream("ab_nat", 1, 1)
            taps(1)
            for f in range(4):
                mark(v.tensor_scalar(SN[:, f, :], SN[:, f, :], oml[:, f:f + 1], None, ALU.mult))
            stream("ab_nat", 2, 1)
            taps(1)
            stream("ab_nat", 3, 1)
            v.wait_ge(hg_ln, 1)
            for f in range(4):
                mark(v.tensor_tensor_scan(HB[:, f, :], cst[:, C_SCAN:C_SCAN + SEQ], LF[:, f, :], 0.0, ALU.mult, ALU.add))
            done(hg_b)
            hb4 = HB.rearrange("p k (n c) -> p (k n) c", c=HG_CHUNK)
            lf4 = LF.rearrange("p k (n c) -> p (k n) c", c=HG_CHUNK)
            mark(v.tensor_tensor(lf4, hb4[:, :, HG_CHUNK - 1:HG_CHUNK].to_broadcast([P, 32, HG_CHUNK]), hb4, ALU.subtract))
            done(hg_b)
            stream("xk0", 0, 1)
            taps(1)
            stream("xk0", 1, 1)
            taps(1)
            v.wait_ge(hg_e, 2)
            v.wait_ge(evacuated, kb + 8)
            mark(v.tensor_tensor(HQ, HQ, SF, ALU.mult))
            stream("xk0", 2, 1)
            mark(v.tensor_tensor(KT, KT, SN, ALU.mult))
            taps(1)
            stream("xk0", 3, 1)
            mark(v.tensor_tensor(LF, LF, SN, ALU.mult))
            done(hg_k)
            v.wait_ge(hgb_in, 16)
            v.wait_ge(evacuated, BANK0["ab_nat"] + 4)
            mark(v.tensor_tensor(GG, GG, HGB.rearrange("p (a b) -> p a b", a=1).to_broadcast([P, 2, 512]), ALU.mult))
            for j in range(4):
                stream("xv0", j, 1)
                taps(2)
            v.wait_ge(hg_st, 1)
            hm = cst[:, C_HG:C_HG + P].rearrange("p (a b) -> p a b", a=1).to_broadcast([P, 4, P])
            v.wait_ge(hg_tr, 1)
            for m in range(2):
                v.tensor_tensor(STM[:, m, :].rearrange("p (a b) -> p a b", b=P),
                                bank[4 + m][:, :].rearrange("p (a b) -> p a b", b=P), hm, ALU.mult).then_inc(hg_sm, 1)
            for n in range(N_CHUNK - 1):
                v.wait_ge(hg_ds, n + 1)
                b = bank[6 + n % 2]
                if n == 0:
                    v.tensor_copy(STATE[:, 1, :], b[:, :]).then_inc(hg_s, 1)
                else:
                    v.wait_ge(hg_s, n)
                    for f in range(4):
                        s = slice(P * f, P * f + P)
                        ins = v.scalar_tensor_tensor(STATE[:, n + 1, s], STATE[:, n, s], decay[:, 8 * f + n:8 * f + n + 1],
                                                     b[:, s], ALU.mult, ALU.add)
                    ins.then_inc(hg_s, 1)
                taps(1)
            taps(CV_K)
            v.wait_ge(diag_used, CV_PE)
            wait_own()
            for j in range(2):
                mark(v.tensor_tensor(CA[:, 2 * j:2 * j + 2, :], CA[:, 2 * j:2 * j + 2, :], tv(bank[j][:, :]), ALU.add))
            done(conv_ready)
            v.wait_ge(hg_on, 2)
            at, w = POW_AT["hg"]
            mark(v.tensor_tensor(SQ, ON, ON, ALU.mult))
            wait_own()
            mark(v.tensor_reduce(pow_in[:, at:at + w], nat[:, 4096:5120].rearrange("p (a b) -> p a b", b=P), AX.X, ALU.add))
            wait_own()
            mark(v.tensor_scalar(pow_in[:, at:at + w], pow_in[:, at:at + w], 1.0 / P, EPS, ALU.mult, ALU.add))
            ask("hg")
            v.wait_ge(cv_mu, 1)
            mark(v.tensor_scalar(CR, bank[4][:, 0:SEQ], 1.0 / B_W, None, ALU.mult))
            wait_own()
            mark(v.tensor_tensor(CA, CA, CR.rearrange("p (a b) -> p a b", a=1).to_broadcast([P, 4, SEQ]), ALU.subtract))
            done(cv_c)
            v.tensor_tensor(CS, CA, CA, ALU.mult).then_inc(cv_c, 1)
            v.wait_ge(pow_done, POW_N["hg"])
            on3 = nat[:, 3072:4096].rearrange("p (a b) -> p a b", b=P)
            r3 = pow_out[:, at:at + w].rearrange("p (a b) -> p a b", b=1).to_broadcast([P, 8, P])
            mark(v.tensor_tensor(on3, on3, r3, ALU.mult))
            wait_own()
            mark(v.tensor_tensor(ON, ON, GG, ALU.mult))
            done(hg_y)
            v.wait_ge(cv_sd, 1)
            mark(v.reciprocal(CR, CR))
            wait_own()
            for f in range(4):
                v.tensor_tensor(CA[:, f, :], CA[:, f, :], CR, ALU.mult).then_inc(cv_x, 1)
            v.wait_ge(hg_yh, 2)
            for j in range(2):
                ins = v.tensor_tensor(yl_[:, 2 * j:2 * j + 2, :], tv(bank[6 + j][:, :]),
                                      yh_[:, 2 * j:2 * j + 2, :].bitcast(F32), ALU.subtract)
            ins.then_inc(hg_yl, 1)
            v.wait_ge(cv_v, 4)
            mark(v.tensor_copy(yh_[:, 4:8, :], CA))
            wait_own()
            v.tensor_tensor(yl_[:, 4:8, :], CA, yh_[:, 4:8, :].bitcast(F32), ALU.subtract).then_inc(conv_lo, 1)
            stream("ab_out", 0, 4)
            residual("ab_out", ALPHA)
            row_stats(hv, "mix0", LN_EPS, False, True)
            normalise(hv, "mix0", False)
            for layer in range(2):
                if layer == 1:
                    stream("xv1", 0, 2)
                    v.wait_ge(pm_out, 1)
                    v.wait_ge(h_ready, 5)
                    for m in range(2):
                        for n in range(2):
                            b = bank[DOWN[2 * m + n]]
                            mark(v.tensor_tensor(nrm[:, m, 512 * n:512 * n + 512], b[:, :], PSC[:, 512 * n:512 * n + 512], ALU.mult))
                    wait_own()
                    for m in range(2):
                        mark(v.scalar_tensor_tensor(hv[:, m], hv[:, m], float(ALPHA), nrm[:, m], ALU.mult, ALU.add))
                    wait_own()
                    row_stats(hv, "mix1", LN_EPS, False)
                    stream("xv1", 2, 2)
                    normalise(hv, "mix1", False)
                split_turned(uh, ul)
                stream(f"xq{layer}")
                attention(f"x{layer}")
                stream(f"xo{layer}")
                v.wait_ge(h_ready, 3 + 3 * layer)
                residual(f"xo{layer}", ALPHA)
                row_stats(hv, f"xa{layer}", LN_EPS, False, True)
                if layer == 0:
                    stream("xk1", 0, 1)
                normalise(hv, f"xa{layer}", False)
                if layer == 0:
                    stream("xk1", 1, 3)
                split_turned(uh, ul)
                ffn(f"ffn{layer}", layer)
                v.wait_ge(h_ready, 4 + 3 * layer)
                residual(f"ffn{layer}", ALPHA)
                row_stats(hv, f"ffn{layer}", LN_EPS, False, True)
                normalise(hv, f"ffn{layer}", False)
                v.wait_ge(ln_in, 32 * (3 + 3 * layer))
                v.wait_ge(nrm_ready, 14 + 6 * layer)
                for m in range(2):
                    mark(v.tensor_tensor(hv[:, m], nrm[:, m], LNG, ALU.mult))
                    wait_own()
                    ins = v.tensor_tensor(hv[:, m], hv[:, m], LNB, ALU.add)
                    if layer == 1 or m == 1:
                        ins.then_inc(h_ready, 1)


def kernel(**inputs):
    import concourse.bacc as _bacc
    from concourse.bass_utils import run_bass_kernel_spmd as _run

    nc = _bacc.Bacc("TRN2", target_bir_lowering=False, num_devices=1)
    consts, poolm = shape_constants()
    arrays = {f"in_{k}": np.ascontiguousarray(v) for k, v in inputs.items()}
    arrays["in_consts"], arrays["in_poolm"] = consts, poolm
    t = {k[3:]: nc.dram_tensor(k, a.shape, mybir.dt.from_np(a.dtype), kind="ExternalInput").ap()
         for k, a in arrays.items()}
    out = nc.dram_tensor("out_0", (1, SEQ, D), F32, kind="ExternalOutput").ap()
    build_program(nc, t, out)
    r = _run(nc, [arrays], core_ids=[0])
    return r.results[0]["out_0"]
```
